# Optimizing a Trainium2 kernel written in Bass

```python
import jax, jax.numpy as jnp
from jax import lax
import numpy as np

D_MODEL = 1024
BATCH = 1
SEQ = 128
DEPTH = 1
DEC_BATCH = 1
DEC_SEQ = 1024
PAST_LEN = 128

GRID_W = 64
CONV_WIDTH = D_MODEL // 2
MLSTM_HEADS = 4
MLSTM_DH = (D_MODEL // 2) // MLSTM_HEADS
MLSTM_W = MLSTM_HEADS * MLSTM_DH
MLSTM_CHUNK = 64
N_DIRS = 2
IN_COLS = 3 * CONV_WIDTH + 4 * MLSTM_W + 2 * N_DIRS * MLSTM_HEADS
PEER_HEADS = 8
PEER_DQ = 256
PEER_NKEYS = 128
PEER_N = PEER_NKEYS * PEER_NKEYS
PEER_TOPK = 16
PEER_BLOCK = 128
EPS = 1e-6

kernel_name = 'hymba_shortconv_bimlstm_peer_dit_step'

def rms_norm(x, g):
    xf = x.astype(jnp.float32)
    y = xf * lax.rsqrt(jnp.mean(xf * xf, axis=-1, keepdims=True) + EPS)
    return (y * g.astype(jnp.float32)).astype(x.dtype)

def ada_mod(cvec, w_ada, b_ada):
    m = jax.nn.silu(cvec) @ w_ada + b_ada
    return jnp.split(m[:, None, :], 6, axis=-1)

def conv3(u, w, b):
    up = jnp.pad(u, ((0, 0), (1, 1), (0, 0)))
    return up[:, :-2] * w[0] + up[:, 1:-1] * w[1] + up[:, 2:] * w[2] + b

def short_conv_group(bg, cg, xg, conv_w, conv_b, on_grid):
    u = cg * xg
    if on_grid:
        n, L, ch = u.shape
        rows = L // GRID_W
        y = conv3(u.reshape(n * rows, GRID_W, ch), conv_w, conv_b).reshape(n, L, ch)
    else:
        y = conv3(u, conv_w, conv_b)
    return bg * y

def mlstm_chunkwise(q, k, v, ig, lf, C0, n0, m0):
    Bn, H, L, Dh = q.shape
    T = MLSTM_CHUNK
    nc = L // T
    tril = jnp.tril(jnp.ones((T, T), dtype=bool))

    def to_chunks(a):
        return jnp.moveaxis(a.reshape((Bn, H, nc, T) + a.shape[3:]), 2, 0)

    def step(carry, inp):
        C, n, m = carry
        qc, kc, vc, ic, fc = inp
        b = jnp.cumsum(fc, axis=-1)
        dmat = jnp.where(tril, b[..., :, None] - b[..., None, :] + ic[..., None, :], -jnp.inf)
        inter = b + m[..., None]
        m_t = jnp.maximum(inter, jnp.max(dmat, axis=-1))
        s = jnp.einsum('bhtd,bhsd->bhts', qc, kc) * jnp.exp(dmat - m_t[..., None])
        a = jnp.exp(inter - m_t)
        num = a[..., None] * jnp.einsum('bhtk,bhkv->bhtv', qc, C) + jnp.einsum('bhts,bhsv->bhtv', s, vc)
        den = a * jnp.einsum('bhtk,bhk->bht', qc, n) + jnp.sum(s, axis=-1)
        h = num / jnp.maximum(jnp.abs(den), jnp.exp(-m_t))[..., None]
        m_new = m_t[..., -1]
        w_s = jnp.exp(b[..., -1:] - b + ic - m_new[..., None])
        decay = jnp.exp(b[..., -1] + m - m_new)
        C_new = decay[..., None, None] * C + jnp.einsum('bhs,bhsk,bhsv->bhkv', w_s, kc, vc)
        n_new = decay[..., None] * n + jnp.einsum('bhs,bhsk->bhk', w_s, kc)
        return (C_new, n_new, m_new), h

    xs = (to_chunks(q), to_chunks(k), to_chunks(v), to_chunks(ig), to_chunks(lf))
    (C, n, m), h = lax.scan(step, (C0, n0, m0), xs)
    h = jnp.moveaxis(h, 0, 2).reshape(Bn, H, L, Dh)
    return h, C, n, m

def mlstm_group(qg, kg, vg, og, igr, fgr, b_igate, b_fgate, g_head, C0, n0, m0):
    Bn, L, _ = qg.shape
    f32 = jnp.float32

    def heads(a):
        return a.reshape(Bn, L, MLSTM_HEADS, MLSTM_DH).transpose(0, 2, 1, 3).astype(f32)

    q = heads(qg) * (MLSTM_DH ** -0.5)
    k = heads(kg)
    v = heads(vg)
    ig = (igr.reshape(Bn, L, N_DIRS, MLSTM_HEADS).astype(f32) + b_igate.astype(f32)).transpose(2, 0, 3, 1)
    lf = jax.nn.log_sigmoid(fgr.reshape(Bn, L, N_DIRS, MLSTM_HEADS).astype(f32) + b_fgate.astype(f32)).transpose(2, 0, 3, 1)
    C0 = C0.astype(f32); n0 = n0.astype(f32); m0 = m0.astype(f32)

    def flip(a):
        return jnp.flip(a, axis=2)

    h_f, Cf, nf, mf = mlstm_chunkwise(q, k, v, ig[0], lf[0], C0[:, 0], n0[:, 0], m0[:, 0])
    h_b, Cb, nb, mb = mlstm_chunkwise(flip(q), flip(k), flip(v), flip(ig[1]), flip(lf[1]),
                                      C0[:, 1], n0[:, 1], m0[:, 1])
    h = h_f + flip(h_b)
    h = h * lax.rsqrt(jnp.mean(h * h, axis=-1, keepdims=True) + EPS) * g_head.astype(f32)[None, :, None, :]
    h = h.transpose(0, 2, 1, 3).reshape(Bn, L, MLSTM_W).astype(qg.dtype) * jax.nn.sigmoid(og)
    return h, jnp.stack([Cf, Cb], axis=1), jnp.stack([nf, nb], axis=1), jnp.stack([mf, mb], axis=1)

def token_mixers(h, w_in, b_igate, b_fgate, conv_w, conv_b, g_mlstm, w_out, C0, n0, m0, on_grid):
    proj = h @ w_in
    cw, mw, g = CONV_WIDTH, MLSTM_W, N_DIRS * MLSTM_HEADS
    cuts = [cw, 2 * cw, 3 * cw, 3 * cw + mw, 3 * cw + 2 * mw, 3 * cw + 3 * mw, 3 * cw + 4 * mw, 3 * cw + 4 * mw + g]
    bg, cg, xg, qg, kg, vg, og, igr, fgr = jnp.split(proj, cuts, axis=-1)
    conv_out = short_conv_group(bg, cg, xg, conv_w, conv_b, on_grid)
    ml_out, Cn, nn_, mn = mlstm_group(qg, kg, vg, og, igr, fgr, b_igate, b_fgate, g_mlstm, C0, n0, m0)
    out = jnp.concatenate([conv_out, ml_out], axis=-1) @ w_out
    return out, Cn, nn_, mn

def peer(h, wq, k1, k2, u_tab, v_tab):
    Bn, L, D = h.shape
    half = PEER_DQ // 2
    toks = h.reshape(-1, PEER_BLOCK, D)

    def block(xb):
        T = xb.shape[0]
        q = (xb @ wq).reshape(T, PEER_HEADS, PEER_DQ)
        s1 = jnp.einsum('thd,kd->thk', q[..., :half], k1).astype(jnp.float32)
        s2 = jnp.einsum('thd,kd->thk', q[..., half:], k2).astype(jnp.float32)
        v1, i1 = lax.top_k(s1, PEER_TOPK)
        v2, i2 = lax.top_k(s2, PEER_TOPK)
        cand = (v1[..., :, None] + v2[..., None, :]).reshape(T, PEER_HEADS, PEER_TOPK * PEER_TOPK)
        vs, flat = lax.top_k(cand, PEER_TOPK)
        e = (jnp.take_along_axis(i1, flat // PEER_TOPK, axis=-1) * PEER_NKEYS
             + jnp.take_along_axis(i2, flat % PEER_TOPK, axis=-1))
        gate = jax.nn.softmax(vs, axis=-1)
        a = jnp.einsum('td,thkd->thk', xb, u_tab[e]).astype(jnp.float32)
        w = (gate * jax.nn.gelu(a, approximate=False)).astype(xb.dtype)
        return jnp.einsum('thk,thkd->td', w, v_tab[e])

    return lax.map(block, toks).reshape(Bn, L, D)

def trunk_layer(x, cvec, w_ada, b_ada, g_norm1, w_in, b_igate, b_fgate, conv_w, conv_b, g_mlstm, w_out,
                g_norm2, peer_wq, peer_k1, peer_k2, peer_u, peer_v, C0, n0, m0, on_grid):
    sh1, sc1, ga1, sh2, sc2, ga2 = ada_mod(cvec, w_ada, b_ada)
    h = rms_norm(x, g_norm1) * (1 + sc1) + sh1
    mix, Cn, nn_, mn = token_mixers(h, w_in, b_igate, b_fgate, conv_w, conv_b, g_mlstm, w_out, C0, n0, m0, on_grid)
    x = x + ga1 * mix
    h = rms_norm(x, g_norm2) * (1 + sc2) + sh2
    x = x + ga2 * peer(h, peer_wq, peer_k1, peer_k2, peer_u, peer_v)
    return x, Cn, nn_, mn

def setup_inputs(seed: int = 0) -> dict:
    key = jax.random.key(seed)
    ks = jax.random.split(key, 24)
    nrm = jax.random.normal
    D = D_MODEL
    f = jnp.float32
    return {
        'x_prompt': nrm(ks[0], (BATCH, SEQ, D), f),
        'x_sample': nrm(ks[1], (DEC_BATCH, DEC_SEQ, D), f),
        'state_C': 0.5 * nrm(ks[2], (DEC_BATCH, DEPTH, N_DIRS, MLSTM_HEADS, MLSTM_DH, MLSTM_DH), f),
        'state_n': 0.5 * nrm(ks[3], (DEC_BATCH, DEPTH, N_DIRS, MLSTM_HEADS, MLSTM_DH), f),
        'state_m': nrm(ks[4], (DEC_BATCH, DEPTH, N_DIRS, MLSTM_HEADS), f),
        'c': nrm(ks[5], (DEC_BATCH, D), f),
        'c_ctx': nrm(ks[6], (D,), f),
        'w_ada': 0.5 * D ** -0.5 * nrm(ks[7], (DEPTH, D, 6 * D), f),
        'b_ada': 0.01 * nrm(ks[8], (DEPTH, 6 * D), f),
        'g_norm1': 1.0 + 0.01 * nrm(ks[9], (DEPTH, D), f),
        'w_in': D ** -0.5 * nrm(ks[10], (DEPTH, D, IN_COLS), f),
        'b_igate': 0.1 * nrm(ks[11], (DEPTH, N_DIRS, MLSTM_HEADS), f),
        'b_fgate': 3.0 + 0.1 * nrm(ks[12], (DEPTH, N_DIRS, MLSTM_HEADS), f),
        'conv_w': 3.0 ** -0.5 * nrm(ks[13], (DEPTH, 3, CONV_WIDTH), f),
        'conv_b': 0.01 * nrm(ks[14], (DEPTH, CONV_WIDTH), f),
        'g_mlstm': 1.0 + 0.01 * nrm(ks[15], (DEPTH, MLSTM_HEADS, MLSTM_DH), f),
        'w_out': D ** -0.5 * nrm(ks[16], (DEPTH, D, D), f),
        'g_norm2': 1.0 + 0.01 * nrm(ks[17], (DEPTH, D), f),
        'peer_wq': D ** -0.5 * nrm(ks[18], (DEPTH, D, PEER_HEADS * PEER_DQ), f),
        'peer_k1': (PEER_DQ // 2) ** -0.5 * nrm(ks[19], (DEPTH, PEER_NKEYS, PEER_DQ // 2), f),
        'peer_k2': (PEER_DQ // 2) ** -0.5 * nrm(ks[20], (DEPTH, PEER_NKEYS, PEER_DQ // 2), f),
        'peer_u': D ** -0.5 * nrm(ks[21], (DEPTH, PEER_N, D), f),
        'peer_v': 0.3 * nrm(ks[22], (DEPTH, PEER_N, D), f),
        'g_final': 1.0 + 0.01 * nrm(ks[23], (D,), f),
    }

def reference(x_prompt, x_sample, state_C, state_n, state_m, c, c_ctx, w_ada, b_ada, g_norm1, w_in,
              b_igate, b_fgate, conv_w, conv_b, g_mlstm, w_out, g_norm2, peer_wq, peer_k1, peer_k2,
              peer_u, peer_v, g_final):
    f32 = jnp.float32
    B = x_prompt.shape[0]
    zC = jnp.zeros((B, N_DIRS, MLSTM_HEADS, MLSTM_DH, MLSTM_DH), f32)
    zn = jnp.zeros((B, N_DIRS, MLSTM_HEADS, MLSTM_DH), f32)
    zm = jnp.zeros((B, N_DIRS, MLSTM_HEADS), f32)
    cctx = c_ctx[None, :]
    xp, xs = x_prompt, x_sample
    Cs, ns, ms = [], [], []
    for l in range(DEPTH):
        lw = (w_ada[l], b_ada[l], g_norm1[l], w_in[l], b_igate[l], b_fgate[l], conv_w[l], conv_b[l],
              g_mlstm[l], w_out[l], g_norm2[l], peer_wq[l], peer_k1[l], peer_k2[l], peer_u[l], peer_v[l])
        xp, Cn, nn_, mn = trunk_layer(xp, cctx, *lw, zC, zn, zm, False)
        Cs.append(Cn); ns.append(nn_); ms.append(mn)
        xs, _, _, _ = trunk_layer(xs, c, *lw, state_C[:, l], state_n[:, l], state_m[:, l], True)
    y_prompt = rms_norm(xp, g_final)
    y_sample = rms_norm(xs, g_final)
    new_C = jnp.stack(Cs, axis=1)
    new_n = jnp.stack(ns, axis=1)
    new_m = jnp.stack(ms, axis=1)
    return (y_prompt, y_sample, new_C, new_n, new_m)


_drawn_inputs = setup_inputs


def setup_inputs(seed=0):
    import zlib

    import numpy as np

    out = dict(_drawn_inputs(seed))
    spreads = {}
    factors = {'state_C': 33.956,
     'state_n': 51.495,
     'state_m': 22.08,
     'g_norm1': 2.841,
     'conv_b': 44.738,
     'g_mlstm': 64.0,
     'g_norm2': 60.64,
     'g_final': 32.042}
    for name, (base, spread) in spreads.items():
        noise = np.random.default_rng([zlib.crc32(name.encode()), seed]).standard_normal(out[name].shape)
        drawn = base * np.exp(spread * noise) if base else spread * noise
        out[name] = __import__('jax').numpy.asarray(drawn.astype(out[name].dtype))
    for name, factor in factors.items():
        out[name] = (out[name] * factor).astype(out[name].dtype)
    return out
```

```python
from contextlib import ExitStack

import concourse.bass as bass
from concourse import mybir

ALU = mybir.AluOpType
ACT = mybir.ActivationFunctionType
F32 = mybir.dt.float32
U32 = mybir.dt.uint32
X = mybir.AxisListType.X

P = 128
D = 1024
KC = D // P
NT = 9
TOK = NT * P
BANK = 512
HEADS = 4
DH = 128
GRID = 64
PH = 8
TOPK = 16
KEYS = 128
EPS = 1e-6
LOW = -1.0e30
DROPPED = -3.0e38
KINDS = 7
CG, XG, BG, Q, K, V, OG = range(KINDS)
SPANS = [(0, 512), (512, 1024), (1024, TOK)]


def carry_wait(nc, t, engine):
    spot = t["carry"]
    if engine == "act":
        nc.scalar.copy(spot[:, 0:1], t["ident"][:, 0:1])
    elif engine == "pool":
        nc.gpsimd.tensor_tensor(spot[:, 1:2], t["ident"][:, 0:1], t["ident"][:, 0:1], ALU.add)
    else:
        nc.vector.memset(spot[:, 2:3], 0.0)


def modulation_stage(nc, ctx, t, ident, started):
    PIECES, SLOTS, PER = 12, 4, 4
    with ExitStack() as own:
        wada = own.enter_context(nc.sbuf_tensor("wada", [P, SLOTS, KC, PER * P], F32))
        cond = own.enter_context(nc.sbuf_tensor("cond", [P, KC, 2], F32))
        silu = own.enter_context(nc.sbuf_tensor("silu", [P, KC, 2], F32))
        bias = own.enter_context(nc.sbuf_tensor("bias", [96, P], F32))
        mod_cols = own.enter_context(nc.sbuf_tensor("mod_cols", [P, 96], F32))
        mod_rows = own.enter_context(nc.sbuf_tensor("mod_rows", [96, P], F32))
        ps_cols = own.enter_context(nc.psum_tensor("ps_cols", [P, 96], F32))
        ps_rows = own.enter_context(nc.psum_tensor("ps_rows", [96, BANK], F32))
        cond_in = ctx.enter_context(nc.semaphore("cond_in"))
        bias_in = ctx.enter_context(nc.semaphore("bias_in"))
        piece_in = [ctx.enter_context(nc.semaphore(f"piece_in{j}")) for j in range(SLOTS)]
        piece_used = ctx.enter_context(nc.semaphore("piece_used"))
        silu_done = ctx.enter_context(nc.semaphore("silu_done"))
        cols_copied = ctx.enter_context(nc.semaphore("cols_copied"))
        rows_ready = ctx.enter_context(nc.semaphore("rows_ready"))
        rows_biased = ctx.enter_context(nc.semaphore("rows_biased"))
        mod_out = ctx.enter_context(nc.semaphore("mod_out"))
        cleared = ctx.enter_context(nc.semaphore("cleared"))
        by_cond = ps_cols[:].rearrange("p (c j) -> p c j", c=2)

        with nc.Block() as block:
            @block.sync
            def _(sp):
                sp.dma_start(cond[:], t["cond"]).then_inc(cond_in, 16)
                sp.dma_start(bias[:], t["b_ada"]).then_inc(bias_in, 16)
                with sp.Fori(0, PIECES // SLOTS) as i:
                    for j in range(SLOTS):
                        sp.wait_ge(piece_used, i * SLOTS + j + 1)
                        sp.dma_start(wada[:, j], t["w_ada"][i * SLOTS + j]).then_inc(piece_in[j], 16)
                sp.wait_ge(rows_biased, 1)
                sp.dma_start(t["mod"], mod_rows[:]).then_inc(mod_out, 16)
                sp.wait_ge(mod_out, 16)

            @block.gpsimd
            def _(pool):
                nc.gpsimd.memset(ident[:], 1.0).then_inc(piece_used, SLOTS)
                pool.drain()
                nc.gpsimd.affine_select(out=ident[:], in_=ident[:], compare_op=ALU.is_equal, fill=0.0,
                                        base=0, pattern=[[-1, P]], channel_multiplier=1).then_inc(started, 1)

            @block.scalar
            def _(act):
                act.wait_ge(cond_in, 16)
                nc.scalar.activation(silu[:], cond[:], ACT.Silu).then_inc(silu_done, 1)
                act.wait_ge(piece_used, SLOTS + PIECES)
                nc.scalar.copy(mod_cols[:], ps_cols[:]).then_inc(cols_copied, 1)

            @block.tensor
            def _(pe):
                pe.wait_ge(silu_done, 1)
                with pe.Fori(0, PIECES // SLOTS) as i:
                    for j in range(SLOTS):
                        pe.wait_ge(piece_in[j], i * 16 + 16)
                        for c in range(PER):
                            for k in range(KC):
                                last = nc.tensor.matmul(by_cond[:, :, i * (SLOTS * PER) + (j * PER + c)],
                                                        wada[:, j, k, c * P:(c + 1) * P], silu[:, k, :],
                                                        start=(k == 0), stop=(k == KC - 1))
                        last.then_inc(piece_used, 1)
                pe.wait_ge(started, 1)
                pe.wait_ge(cols_copied, 1)
                nc.tensor.transpose(ps_rows[:, 0:P], mod_cols[:], ident[:]).then_inc(rows_ready, 1)

            @block.vector
            def _(dve):
                dve.wait_ge(bias_in, 16)
                dve.wait_ge(rows_ready, 1)
                nc.vector.tensor_tensor(mod_rows[:], ps_rows[:, 0:P], bias[:], ALU.add).then_inc(rows_biased, 1)


def mod_vector(t, cond, v):
    rows = t["mod"].rearrange("(c v e) p -> c v (e p)", c=2, v=6)
    return rows[cond, v].partition_broadcast(P)


def norm_stage(nc, ctx, t, ident, hT, started):
    SL = 3
    with ExitStack() as own:
        xt = own.enter_context(nc.sbuf_tensor("xt", [P, SL, D], F32))
        ht = own.enter_context(nc.sbuf_tensor("ht", [P, SL, D], F32))
        st = own.enter_context(nc.sbuf_tensor("st", [P, SL, 4], F32))
        gain = own.enter_context(nc.sbuf_tensor("gain", [P, 2, D], F32))
        shift = own.enter_context(nc.sbuf_tensor("shift", [P, 2, D], F32))
        g1 = own.enter_context(nc.sbuf_tensor("g1", [P, D], F32))
        ps = [own.enter_context(nc.psum_tensor(f"psn{j}", [P, 2 * BANK], F32)) for j in range(SL)]
        vec_in = ctx.enter_context(nc.semaphore("vec_in"))
        x_in = [ctx.enter_context(nc.semaphore(f"x_in{j}")) for j in range(SL)]
        meansq = ctx.enter_context(nc.semaphore("meansq"))
        rooted = ctx.enter_context(nc.semaphore("rooted"))
        normed = ctx.enter_context(nc.semaphore("normed"))
        turned = ctx.enter_context(nc.semaphore("turned"))
        evicted = ctx.enter_context(nc.semaphore("evicted"))

        with nc.Block() as block:
            @block.sync
            def _(sp):
                sp.dma_start(g1[:], t["g_norm1"].partition_broadcast(P)).then_inc(vec_in, 16)
                for c in range(2):
                    sp.dma_start(shift[:, c], mod_vector(t, c, 0)).then_inc(vec_in, 16)
                    sp.dma_start(gain[:, c], mod_vector(t, c, 1)).then_inc(vec_in, 16)
                with sp.Fori(0, NT // SL) as i:
                    for j in range(SL):
                        sp.wait_ge(normed, i * SL + j + 1)
                        sp.dma_start(xt[:, j], t["x"][i * SL + j]).then_inc(x_in[j], 16)

            @block.vector
            def _(dve):
                nc.vector.memset(st[:], 0.0).then_inc(normed, SL)
                dve.wait_ge(vec_in, 5 * 16)
                for c in range(2):
                    nc.vector.scalar_tensor_tensor(out=gain[:, c], in0=gain[:, c], scalar=1.0, in1=g1[:],
                                                   op0=ALU.add, op1=ALU.mult)
                dve.drain()
                with dve.Fori(0, NT // SL) as i:
                    for j in range(SL):
                        tile = i * SL + j
                        dve.wait_ge(x_in[j], i * 16 + 16)
                        dve.wait_ge(turned, i * SL + j + 1)
                        nc.vector.tensor_tensor_reduce(out=ht[:, j], in0=xt[:, j], in1=xt[:, j], scale=1.0,
                                                       scalar=0.0, op0=ALU.mult, op1=ALU.add,
                                                       accum_out=st[:, j, 0:1])
                        dve.drain()
                        nc.vector.tensor_scalar(st[:, j, 1:2], st[:, j, 0:1], 1.0 / D, EPS, ALU.mult,
                                                ALU.add).then_inc(meansq, 1)
                        dve.wait_ge(rooted, tile + 1)
                        nc.vector.reciprocal(st[:, j, 3:4], st[:, j, 2:3])
                        dve.drain()
                        nc.vector.scalar_tensor_tensor(out=ht[:, j], in0=xt[:, j], scalar=st[:, j, 3:4],
                                                       in1=gain[:, (tile + 7) // 8], op0=ALU.mult, op1=ALU.mult)
                        dve.drain()
                        nc.vector.tensor_tensor(ht[:, j], ht[:, j], shift[:, (tile + 7) // 8],
                                                ALU.add).then_inc(normed, 1)

            @block.scalar
            def _(act):
                with act.Fori(0, NT // SL) as i:
                    for j in range(SL):
                        act.wait_ge(meansq, i * SL + j + 1)
                        nc.scalar.activation(st[:, j, 2:3], st[:, j, 1:2], ACT.Sqrt).then_inc(rooted, 1)
                        act.drain()
                        act.wait_ge(turned, i * SL + j + 1 + SL)
                        carry_wait(nc, t, "act")
                        nc.scalar.copy(hT[:, :, bass.ts(i * SL + j, P)],
                                       ps[j][:].rearrange("p (k n) -> p k n", k=KC)).then_inc(evicted, 1)

            @block.gpsimd
            def _(pool):
                nc.gpsimd.memset(t["junk"][:, 0:1], 0.0).then_inc(turned, SL)
                nc.gpsimd.memset(t["junk"][:, 1:2], 0.0).then_inc(evicted, SL)

            @block.tensor
            def _(pe):
                with pe.Fori(0, NT // SL) as i:
                    for j in range(SL):
                        pe.wait_ge(normed, i * SL + j + 1 + SL)
                        pe.wait_ge(evicted, i * SL + j + 1)
                        for k in range(KC):
                            last = nc.tensor.transpose(ps[j][:, k * P:(k + 1) * P], ht[:, j, k * P:(k + 1) * P],
                                                       ident[:])
                        last.then_inc(turned, 1)


def gates_stage(nc, ctx, t, ident, hT, neg_u, decay, cols, masks):
    with ExitStack() as own:
        wg = own.enter_context(nc.sbuf_tensor("wg", [P, KC, 16], F32))
        gb = own.enter_context(nc.sbuf_tensor("gb", [HEADS, 4], F32))
        m0 = own.enter_context(nc.sbuf_tensor("m0", [HEADS, 2], F32))
        keep = own.enter_context(nc.sbuf_tensor("keep", [HEADS, TOK], F32))
        low = own.enter_context(nc.sbuf_tensor("low", [HEADS, TOK], F32))
        gi = own.enter_context(nc.sbuf_tensor("gi", [HEADS, TOK], F32))
        gf = own.enter_context(nc.sbuf_tensor("gf", [HEADS, TOK], F32))
        lg = own.enter_context(nc.sbuf_tensor("lg", [HEADS, TOK], F32))
        bsum = own.enter_context(nc.sbuf_tensor("bsum", [HEADS, TOK], F32))
        gmb = own.enter_context(nc.sbuf_tensor("gmb", [HEADS, 2, TOK], F32))
        top = own.enter_context(nc.sbuf_tensor("top", [HEADS, TOK], F32))
        em = own.enter_context(nc.sbuf_tensor("em", [HEADS, 2, TOK], F32))
        ends = own.enter_context(nc.sbuf_tensor("ends", [HEADS, 3, NT], F32))
        newm = own.enter_context(nc.sbuf_tensor("newm", [HEADS, 2], F32))
        ps = [own.enter_context(nc.psum_tensor(f"psg{j}", [P, 3 * BANK], F32)) for j in range(2)]
        ps_cols = own.enter_context(nc.psum_tensor("psgc", [P, BANK], F32))
        g_in = ctx.enter_context(nc.semaphore("g_in"))
        g_proj = ctx.enter_context(nc.semaphore("g_proj"))
        g_taken = ctx.enter_context(nc.semaphore("g_taken"))
        g_forget = ctx.enter_context(nc.semaphore("g_forget"))
        g_log = ctx.enter_context(nc.semaphore("g_log"))
        g_args = ctx.enter_context(nc.semaphore("g_args"))
        g_exp = ctx.enter_context(nc.semaphore("g_exp"))
        g_cols = ctx.enter_context(nc.semaphore("g_cols"))
        g_masks = ctx.enter_context(nc.semaphore("g_masks"))
        g_out = ctx.enter_context(nc.semaphore("g_out"))
        chunks = lambda a: a.rearrange("h (c n) -> h c n", c=NT)

        with nc.Block() as block:
            @block.sync
            def _(sp):
                sp.dma_start(wg[:], t["w_gate"]).then_inc(g_in, 16)
                sp.dma_start(gb[:], t["b_gate"]).then_inc(g_in, 16)
                sp.dma_start(m0[:], t["m0"]).then_inc(g_in, 16)
                sp.wait_ge(g_args, 2)
                sp.dma_start(t["new_m"], newm[:]).then_inc(g_out, 16)
                sp.wait_ge(g_out, 16)

            @block.gpsimd
            def _(pool):
                nc.gpsimd.memset(masks[:], 1.0)
                pool.drain()
                nc.gpsimd.affine_select(out=masks[:, 0], in_=masks[:, 0], compare_op=ALU.is_ge, fill=0.0,
                                        base=0, pattern=[[1, P]], channel_multiplier=-1)
                nc.gpsimd.affine_select(out=masks[:, 1], in_=masks[:, 1], compare_op=ALU.is_ge, fill=0.0,
                                        base=0, pattern=[[-1, P]], channel_multiplier=1).then_inc(g_masks, 1)

            @block.tensor
            def _(pe):
                pe.wait_ge(g_in, 48)
                for d in range(2):
                    for which in range(2):
                        if d:
                            pe.wait_ge(g_taken, which + 1)
                        g = which * 2 + d
                        for a, b in SPANS:
                            for k in range(KC):
                                last = nc.tensor.matmul(ps[which][0:HEADS, a:b], wg[:, k, g * 4:g * 4 + 4],
                                                        hT[:, k, a:b], start=(k == 0), stop=(k == KC - 1))
                        last.then_inc(g_proj, 1)
                for d in range(2):
                    pe.wait_ge(g_args, d + 1)
                    pe.wait_ge(g_exp, d + 1)
                    for kind, rows in enumerate((gmb, em)):
                        for c in range(NT):
                            at = ((d * 2 + kind) * NT + c) * HEADS
                            last = nc.tensor.transpose(ps_cols[:, at:at + HEADS],
                                                       rows[:, d, c * P:(c + 1) * P],
                                                       ident[0:HEADS, 0:HEADS])
                last.then_inc(g_cols, 1)

            @block.scalar
            def _(act):
                for d in range(2):
                    act.wait_ge(g_forget, d + 1)
                    nc.scalar.activation(lg[:], gf[:], ACT.Abs)
                    act.drain()
                    nc.scalar.activation(lg[:], lg[:], ACT.Exp, scale=-1.0)
                    act.drain()
                    nc.scalar.activation(lg[:], lg[:], ACT.Ln, bias=1.0).then_inc(g_log, 1)
                    act.wait_ge(g_args, d + 1)
                    nc.scalar.activation(decay[:, d], decay[:, d], ACT.Exp)
                    nc.scalar.activation(em[:, d], em[:, d], ACT.Exp).then_inc(g_exp, 1)
                act.wait_ge(g_cols, 1)
                nc.scalar.copy(cols[:].rearrange("p a b c h -> p (a b c h)"), ps_cols[:, 0:16 * NT])

            @block.vector
            def _(dve):
                nc.vector.memset(keep[:], 1.0)
                nc.vector.memset(low[:], 0.0)
                nc.vector.memset(ends[:], 0.0)
                dve.drain()
                nc.vector.memset(chunks(keep[:])[:, :, 0:1], 0.0)
                nc.vector.memset(chunks(low[:])[:, :, 0:1], LOW)
                dve.wait_ge(g_in, 48)
                dve.drain()
                for d in range(2):
                    run = (lambda a: a) if d == 0 else (lambda a: a[:, ::-1])
                    end = P - 1 if d == 0 else 0
                    dve.wait_ge(g_proj, 2 * d + 1)
                    nc.vector.tensor_scalar(gi[:], ps[0][0:HEADS, 0:TOK], gb[:, d:d + 1], None,
                                            ALU.add).then_inc(g_taken, 1)
                    dve.wait_ge(g_proj, 2 * d + 2)
                    nc.vector.tensor_scalar(gf[:], ps[1][0:HEADS, 0:TOK], gb[:, 2 + d:3 + d], None,
                                            ALU.add).then_inc(g_taken, 1)
                    dve.drain()
                    nc.vector.memset(ends[:, 2, 0:1], 0.0).then_inc(g_forget, 1)
                    dve.wait_ge(g_log, d + 1)
                    nc.vector.scalar_tensor_tensor(out=gf[:], in0=gf[:], scalar=0.0, in1=lg[:],
                                                   op0=ALU.min, op1=ALU.subtract)
                    dve.drain()
                    nc.vector.tensor_tensor_scan(out=run(bsum[:]), data0=keep[:], data1=run(gf[:]), initial=0.0,
                                                 op0=ALU.mult, op1=ALU.add)
                    dve.drain()
                    nc.vector.tensor_tensor(gmb[:, d], gi[:], bsum[:], ALU.subtract)
                    dve.drain()
                    nc.vector.tensor_tensor_scan(out=run(top[:]), data0=low[:], data1=run(gmb[:, d]), initial=0.0,
                                                 op0=ALU.add, op1=ALU.max)
                    dve.drain()
                    nc.vector.tensor_copy(ends[:, 0], chunks(top[:])[:, :, end])
                    nc.vector.tensor_copy(ends[:, 1], chunks(bsum[:])[:, :, end])
                    first = 1 if d == 0 else NT - 1
                    nc.vector.tensor_copy(ends[:, 2, first:first + 1], m0[:, d:d + 1])
                    dve.drain()
                    nc.vector.scalar_tensor_tensor(out=newm[:, d:d + 1], in0=ends[:, 0, 0:1], scalar=0.0,
                                                   in1=ends[:, 1, 0:1], op0=ALU.max, op1=ALU.add)
                    src = slice(1, NT - 1) if d == 0 else slice(NT - 1, 1, -1)
                    dst = slice(2, NT) if d == 0 else slice(NT - 2, 0, -1)
                    nc.vector.tensor_tensor_scan(out=ends[:, 2, dst], data0=ends[:, 0, src], data1=ends[:, 1, src],
                                                 initial=m0[:, d:d + 1], op0=ALU.max, op1=ALU.add)
                    dve.drain()
                    before = ends[:, 2, :].unsqueeze(2).to_broadcast([HEADS, NT, P])
                    nc.vector.tensor_tensor(chunks(top[:]), chunks(top[:]), before, ALU.max)
                    dve.drain()
                    nc.vector.tensor_scalar(neg_u[:, d], top[:], -1.0, None, ALU.mult)
                    nc.vector.tensor_tensor(chunks(decay[:, d]), before, chunks(top[:]), ALU.subtract)
                    dve.drain()
                    nc.vector.tensor_tensor(em[:, d], neg_u[:, d], bsum[:], ALU.subtract).then_inc(g_args, 1)
                    dve.drain()


JOBS = ["q", "k", "v", "ktok", "vtok", "s", "u0", "a0", "og", "kv0", "cg", "num0", "u1", "a1", "xg", "kv1",
        "bg", "num1", "hT"]
NJ = len(JOBS)
PROJ = {"cg": CG, "xg": XG, "bg": BG, "q": Q, "k": K, "v": V, "og": OG}
IN_REGION = [(NJ + 1) // 2, NJ // 2]


def job_done(h, name):
    return h * NJ + (JOBS.index(name) + 1 + NJ)


def evicted(h, name):
    r, value = region_free(h, name)
    return r, value + 1


def region_free(h, name):
    j = JOBS.index(name)
    return j % 2, h * IN_REGION[j % 2] + (j // 2 + 1)


def mixer_stage(nc, ctx, t, ident, hT, catT, neg_u, decay, cols, masks, started):
    W = DH + 1
    with ExitStack() as own:
        def sb(name, shape):
            return own.enter_context(nc.sbuf_tensor(name, shape, F32))

        def sem(name):
            return ctx.enter_context(nc.semaphore(name))

        w = sb("w", [P, KINDS, KC, P])
        qT, kT, vT, og = (sb(n, [P, TOK]) for n in ("qT", "kT", "vT", "ogT"))
        ktok = sb("ktok", [P, NT, P])
        vtok = sb("vtok", [P, NT, W])
        sT = sb("sT", [P, NT, P])
        seen = sb("seen", [P, NT, P])
        qa = sb("qa", [P, NT, P])
        kw = sb("kw", [P, NT, P])
        states = sb("states", [P, NT, W])
        num = sb("num", [P, NT, W])
        hsum = sb("hsum", [P, NT, P])
        u = sb("u", [P, TOK])
        y = sb("y", [P, TOK])
        dec = sb("dec", [P, NT])
        den = sb("den", [P, 2, NT])
        rows = sb("rows", [HEADS, 2, TOK])
        ones = sb("ones", [HEADS, P])
        new = sb("new", [P, 2, W])
        conv = sb("conv", [P, 4, 4])
        gm = sb("gm", [P, HEADS])
        region = [own.enter_context(nc.psum_tensor(f"region{r}", [P, 3 * BANK], F32)) for r in range(2)]

        w_in = [sem(f"w_in{k}") for k in range(KINDS)]
        small_in = sem("small_in")
        jobs_done, free = sem("jobs_done"), [sem("region_free0"), sem("region_free1")]
        masked, exped = sem("masked"), sem("exped")
        weighted, ready = sem("k_weighted"), sem("seen_ready")
        h_ready, rooted = sem("h_ready"), sem("h_rooted")
        meansq, state_in = sem("h_meansq"), [sem("state_in0"), sem("state_in1")]
        new_ready, new_out = sem("new_ready"), [sem("new_out0"), sem("new_out1")]
        combined = sem("combined")

        def wait_evicted(eng, h, name):
            r, value = evicted(h, name)
            eng.wait_ge(free[r], value)

        def reg(name):
            return region[JOBS.index(name) % 2]

        def toks(name):
            return reg(name)[:, 0:TOK]

        def tiles(name):
            return reg(name)[:, 0:TOK].rearrange("p (c n) -> p c n", c=NT)

        def wide(name):
            return reg(name)[:].rearrange("p (b n) -> p b n", b=3)[:, :, 0:3 * W].rearrange(
                "p b (c n) -> p b c n", c=3)

        def wide_at(name, c):
            return reg(name)[:, (c // 3) * BANK + (c % 3) * W:(c // 3) * BANK + (c % 3 + 1) * W]

        with nc.Block() as block:
            @block.sync
            def _(sp):
                sp.dma_start(conv[:], t["conv"]).then_inc(small_in, 16)
                sp.dma_start(gm[:], t["g_mlstm"]).then_inc(small_in, 16)
                sp.dma_start(states[:, 1], t["state"][0, 0]).then_inc(state_in[0], 16)

                def store_new(h, d):
                    sp.wait_ge(new_ready, h * 2 + (d + 1))
                    sp.dma_start(t["new_C"][d, h], new[:, d, 0:DH]).then_inc(new_out[d], 16)
                    sp.dma_start(t["new_n"][d, h], new[:, d, DH:W]).then_inc(new_out[d], 16)

                for h in range(HEADS + 1):
                    for name in JOBS:
                        if name in PROJ and h < HEADS:
                            sp.wait_ge(jobs_done, h * NJ + (JOBS.index(name) + 1))
                            sp.dma_start(w[:, PROJ[name]], t["w_in"][h, PROJ[name]]).then_inc(w_in[PROJ[name]], 16)
                        if h == 0:
                            continue
                        if name in ("kv0", "kv1"):
                            store_new(h - 1, int(name[-1]))
                        elif name == "num0":
                            sp.wait_ge(jobs_done, job_done(h - 1, "num0"))
                            sp.dma_start(states[:, NT - 1], t["state"][1, h - 1]).then_inc(state_in[1], 16)
                        elif name == "num1" and h < HEADS:
                            sp.wait_ge(jobs_done, job_done(h - 1, "num1"))
                            sp.dma_start(states[:, 1], t["state"][0, h]).then_inc(state_in[0], 16)
                for d in range(2):
                    sp.wait_ge(new_out[d], 32 + 32 * HEADS)

            @block.gpsimd
            def _(pool):
                nc.gpsimd.memset(ones[:], 1.0).then_inc(jobs_done, NJ)
                nc.gpsimd.memset(vtok[:, :, DH:W], 1.0).then_inc(free[0], 1)
                nc.gpsimd.memset(t["junk"][:, 0:1], 1.0).then_inc(free[1], 1)
                for d in range(2):
                    nc.gpsimd.memset(t["junk"][:, 1 + d:2 + d], 1.0).then_inc(new_out[d], 32)

            @block.tensor
            def _(pe):
                with pe.Fori(0, HEADS) as h:
                    def take(name):
                        r, value = region_free(h, name)
                        pe.wait_ge(free[r], value)

                    def project(name):
                        pe.wait_ge(w_in[PROJ[name]], h * 16 + 16)
                        take(name)
                        for k in range(KC):
                            for a, b in SPANS:
                                last = nc.tensor.matmul(reg(name)[:, a:b], w[:, PROJ[name], k, :], hT[:, k, a:b],
                                                        start=(k == 0), stop=(k == KC - 1))
                        last.then_inc(jobs_done, 1)

                    def turn(name, src):
                        for c in range(NT):
                            last = nc.tensor.transpose(tiles(name)[:, c], src[:, c * P:(c + 1) * P], ident[:])
                        last.then_inc(jobs_done, 1)

                    for name in ("q", "k", "v"):
                        project(name)
                    wait_evicted(pe, h, "q")
                    wait_evicted(pe, h, "k")
                    take("ktok")
                    turn("ktok", kT)
                    wait_evicted(pe, h, "v")
                    take("vtok")
                    turn("vtok", vT)
                    take("s")
                    for c in range(NT):
                        last = nc.tensor.matmul(tiles("s")[:, c], kT[:, c * P:(c + 1) * P], qT[:, c * P:(c + 1) * P],
                                                start=True, stop=True)
                    last.then_inc(jobs_done, 1)

                    def spread_rows(d):
                        pe.wait_ge(masked, h * 2 + (d + 1))
                        for kind, name in enumerate((f"u{d}", f"a{d}")):
                            take(name)
                            for a, b in SPANS:
                                last = nc.tensor.matmul(reg(name)[:, a:b], ones[:], rows[:, kind, a:b],
                                                        start=True, stop=True)
                            last.then_inc(jobs_done, 1)

                    def outer(d):
                        pe.wait_ge(weighted, h * 2 + (d + 1))
                        take(f"kv{d}")
                        for c in range(NT):
                            last = nc.tensor.matmul(wide_at(f"kv{d}", c), kw[:, c, :], vtok[:, c, :],
                                                    start=True, stop=True)
                        last.then_inc(jobs_done, 1)

                    def numerators(d):
                        pe.wait_ge(ready, h * 2 + (d + 1))
                        wait_evicted(pe, h, "vtok")
                        wait_evicted(pe, h, f"kv{d}")
                        take(f"num{d}")
                        for c in range(NT):
                            last = nc.tensor.matmul(wide_at(f"num{d}", c), seen[:, c, :], vtok[:, c, :],
                                                    start=True, stop=(c == 0))
                            if c:
                                last = nc.tensor.matmul(wide_at(f"num{d}", c), qa[:, c, :], states[:, c, :],
                                                        start=False, stop=True)
                        last.then_inc(jobs_done, 1)

                    spread_rows(0)
                    project("og")
                    outer(0)
                    project("cg")
                    numerators(0)
                    spread_rows(1)
                    project("xg")
                    outer(1)
                    project("bg")
                    numerators(1)
                    pe.wait_ge(h_ready, h + 1)
                    take("hT")
                    for c in range(NT):
                        last = nc.tensor.transpose(tiles("hT")[:, c], hsum[:, c, :], ident[:])
                    last.then_inc(jobs_done, 1)

            @block.scalar
            def _(act):
                with act.Fori(0, HEADS) as h:
                    def evict(name, out, src, func=ACT.Copy, scale=1.0):
                        act.wait_ge(jobs_done, job_done(h, name))
                        nc.scalar.activation(out, src, func, scale=scale).then_inc(free[JOBS.index(name) % 2], 1)

                    evict("q", qT[:], toks("q"), scale=float(DH) ** -0.5)
                    evict("k", kT[:], toks("k"))
                    evict("v", vT[:], toks("v"))
                    evict("ktok", ktok[:], tiles("ktok"))
                    evict("vtok", vtok[:, :, 0:DH], tiles("vtok"))
                    evict("s", sT[:], tiles("s"))

                    def exps(d):
                        wait_evicted(act, h, f"u{d}")
                        nc.scalar.activation(seen[:], seen[:], ACT.Exp).then_inc(exped, 1)
                        evict(f"a{d}", qa[:], tiles(f"a{d}"))

                    def copy_num(d):
                        if d:
                            act.wait_ge(combined, h * 2 + 2 + 1)
                        act.wait_ge(jobs_done, job_done(h, f"num{d}"))
                        for b in range(3):
                            last = nc.scalar.copy(num[:, 3 * b:3 * b + 3, :], wide(f"num{d}")[:, b])
                        last.then_inc(free[JOBS.index(f"num{d}") % 2], 1)

                    exps(0)
                    evict("og", og[:], toks("og"), func=ACT.Sigmoid)
                    evict("cg", u[:], toks("cg"))
                    copy_num(0)
                    exps(1)
                    copy_num(1)
                    act.wait_ge(meansq, h + 1)
                    nc.scalar.activation(den[:, 1, :], den[:, 0, :], ACT.Sqrt).then_inc(rooted, 1)

            @block.vector
            def _(dve):
                nc.vector.memset(t["tock"][:, 0:2], 0.0).then_inc(combined, 2)
                dve.wait_ge(small_in, 32)
                with dve.Fori(0, HEADS) as h:
                    def mask_rows(d):
                        if d:
                            dve.wait_ge(jobs_done, job_done(h, "a0"))
                        for kind, src in enumerate((neg_u, decay)):
                            last = nc.vector.tensor_scalar(rows[:, kind], src[:, d], ident[0:HEADS, bass.ds(h, 1)],
                                                           None, ALU.mult)
                        last.then_inc(masked, 1)

                    def arguments(d):
                        dve.wait_ge(jobs_done, job_done(h, f"u{d}"))
                        for c in range(NT):
                            last = nc.vector.tensor_scalar(seen[:, c, :], tiles(f"u{d}")[:, c],
                                                           cols[:, d, 0, c, bass.ds(h, 1)], 0.0, ALU.add, ALU.min)
                        last.then_inc(free[JOBS.index(f"u{d}") % 2], 1)

                    def weights(d):
                        end = P - 1 if d == 0 else 0
                        dve.wait_ge(exped, h * 2 + (d + 1))
                        wait_evicted(dve, h, "ktok")
                        wait_evicted(dve, h, f"a{d}")
                        nc.vector.tensor_copy(dec[:], qa[:, :, end])
                        nc.vector.tensor_tensor(kw[:], ktok[:], seen[:, :, end:end + 1].to_broadcast([P, NT, P]),
                                                ALU.mult).then_inc(weighted, 1)
                        dve.drain()
                        nc.vector.tensor_tensor(qa[:], qa[:], qT[:].rearrange("p (c n) -> p c n", c=NT), ALU.mult)
                        nc.vector.tensor_tensor(seen[:], seen[:],
                                                masks[:, d, :].unsqueeze(1).to_broadcast([P, NT, P]), ALU.mult)
                        dve.drain()
                        nc.vector.tensor_tensor(seen[:], seen[:], sT[:], ALU.mult).then_inc(ready, 1)

                    def chain(d):
                        dve.wait_ge(state_in[d], h * 16 + 16)
                        dve.wait_ge(jobs_done, job_done(h, f"kv{d}"))
                        dve.wait_ge(new_out[d], h * 32 + 32)
                        nc.vector.tensor_copy(new[:, d], wide_at(f"kv{d}", 0)).then_inc(new_ready, 1)
                        order = list(range(1, NT - 1)) if d == 0 else list(range(NT - 1, 1, -1))
                        for c in order:
                            last = nc.vector.scalar_tensor_tensor(out=states[:, c + 1 if d == 0 else c - 1],
                                                           in0=states[:, c], scalar=dec[:, c:c + 1],
                                                           in1=wide_at(f"kv{d}", c), op0=ALU.mult, op1=ALU.add)
                            if c == order[-1]:
                                last.then_inc(free[JOBS.index(f"kv{d}") % 2], 1)
                            dve.drain()

                    def combine(d):
                        wait_evicted(dve, h, f"num{d}")
                        nc.vector.scalar_tensor_tensor(out=den[:, 0, :], in0=num[:, :, DH], scalar=-1.0,
                                                       in1=num[:, :, DH], op0=ALU.mult, op1=ALU.max)
                        dve.drain()
                        nc.vector.tensor_tensor(den[:, 0, :], den[:, 0, :], cols[:, d, 1, :, h], ALU.max)
                        dve.drain()
                        nc.vector.reciprocal(den[:, 1, :], den[:, 0, :])
                        dve.drain()
                        r = den[:, 1, :].unsqueeze(2).to_broadcast([P, NT, P])
                        if d == 0:
                            nc.vector.tensor_tensor(hsum[:], num[:, :, 0:DH], r, ALU.mult).then_inc(combined, 1)
                        else:
                            nc.vector.tensor_tensor(num[:, :, 0:DH], num[:, :, 0:DH], r, ALU.mult)
                            dve.drain()
                            nc.vector.tensor_tensor(hsum[:], hsum[:], num[:, :, 0:DH], ALU.add)\
                                .then_inc(combined, 1)
                        dve.drain()

                    mask_rows(0)
                    arguments(0)
                    weights(0)
                    mask_rows(1)
                    chain(0)
                    combine(0)
                    arguments(1)
                    weights(1)

                    dve.wait_ge(jobs_done, job_done(h, "xg"))
                    nc.vector.tensor_tensor(u[:], toks("xg"), u[:], ALU.mult)\
                        .then_inc(free[JOBS.index("xg") % 2], 1)
                    dve.drain()
                    nc.vector.tensor_scalar(y[:], u[:], conv[:, h, 1:2], conv[:, h, 3:4], ALU.mult, ALU.add)
                    dve.drain()
                    for tap, (to, frm) in ((0, (slice(1, None), slice(0, -1))), (2, (slice(0, -1), slice(1, None)))):
                        for a, b, n in ((0, P, P), (P, TOK, GRID)):
                            yr = y[:, a:b].rearrange("p (r n) -> p r n", n=n)
                            ur = u[:, a:b].rearrange("p (r n) -> p r n", n=n)
                            nc.vector.scalar_tensor_tensor(out=yr[:, :, to], in0=ur[:, :, frm],
                                                           scalar=conv[:, h, tap:tap + 1], in1=yr[:, :, to],
                                                           op0=ALU.mult, op1=ALU.add)
                        dve.drain()
                    chain(1)
                    dve.wait_ge(jobs_done, job_done(h, "bg"))
                    nc.vector.tensor_tensor(catT[:, h, :], toks("bg"), y[:], ALU.mult)\
                        .then_inc(free[JOBS.index("bg") % 2], 1)

                    combine(1)
                    nc.vector.tensor_tensor(kw[:], hsum[:], hsum[:], ALU.mult)
                    dve.drain()
                    nc.vector.tensor_reduce(den[:, 1, :], kw[:], X, ALU.add)
                    dve.drain()
                    nc.vector.tensor_scalar(den[:, 0, :], den[:, 1, :], 1.0 / DH, EPS, ALU.mult, ALU.add)\
                        .then_inc(meansq, 1)
                    dve.wait_ge(rooted, h + 1)
                    nc.vector.reciprocal(den[:, 0, :], den[:, 1, :])
                    dve.drain()
                    nc.vector.tensor_tensor(hsum[:], hsum[:], den[:, 0, :].unsqueeze(2).to_broadcast([P, NT, P]),
                                            ALU.mult).then_inc(h_ready, 1)
                    dve.wait_ge(jobs_done, job_done(h, "hT"))
                    nc.vector.scalar_tensor_tensor(out=catT[:, h + 4, :], in0=toks("hT"), scalar=gm[:, bass.ds(h, 1)],
                                                   in1=og[:], op0=ALU.mult, op1=ALU.mult)\
                        .then_inc(free[JOBS.index("hT") % 2], 1)


def output_stage(nc, ctx, t, ident, catT, started):
    SL = 3
    with ExitStack() as own:
        def sb(name, shape):
            return own.enter_context(nc.sbuf_tensor(name, shape, F32))

        def sem(name):
            return ctx.enter_context(nc.semaphore(name))

        wo = sb("wo", [P, KC, D])
        cat = sb("cat", [P, SL, KC, P])
        xt, x1, h2 = sb("o_x", [P, SL, D]), sb("o_x1", [P, SL, D]), sb("o_h2", [P, SL, D])
        h2T = sb("o_h2T", [P, SL, KC, P])
        gate, gain, shift, g2 = sb("o_gate", [P, 2, D]), sb("o_gain", [P, 2, D]), sb("o_shift", [P, 2, D]), sb("o_g2", [P, D])
        st = sb("o_st", [P, SL, 4])
        mix = [own.enter_context(nc.psum_tensor(f"mix{j}", [P, 2 * BANK], F32)) for j in range(SL)]
        ps_t = own.enter_context(nc.psum_tensor("o_t", [P, 2 * BANK], F32))
        vec_in, wo_in = sem("o_vec_in"), sem("wo_in")
        x_in = [sem(f"o_x_in{j}") for j in range(SL)]
        cut, mixed, added = sem("cat_cut"), sem("mixed"), sem("added")
        meansq, rooted, normed = sem("o_meansq"), sem("o_rooted"), sem("o_normed")
        turned, evicted = sem("o_turned"), sem("o_evicted")
        stored = [sem(f"o_stored{j}") for j in range(SL)]
        tail = sem("o_tail")

        with nc.Block() as block:
            @block.sync
            def _(sp):
                sp.dma_start(wo[:], t["w_out"]).then_inc(wo_in, 16)
                sp.dma_start(g2[:], t["g_norm2"].partition_broadcast(P)).then_inc(vec_in, 16)
                for c in range(2):
                    sp.dma_start(gate[:, c], mod_vector(t, c, 2)).then_inc(vec_in, 16)
                    sp.dma_start(shift[:, c], mod_vector(t, c, 3)).then_inc(vec_in, 16)
                    sp.dma_start(gain[:, c], mod_vector(t, c, 4)).then_inc(vec_in, 16)
                with sp.Fori(0, NT // SL) as i:
                    for j in range(SL):
                        sp.wait_ge(added, i * SL + j + 1)
                        sp.dma_start(xt[:, j], t["x"][i * SL + j]).then_inc(x_in[j], 16)
                    for j in range(SL):
                        tile = i * SL + j
                        sp.wait_ge(normed, tile + 1)
                        sp.dma_start(t["x1"][tile], x1[:, j]).then_inc(stored[j], 16)
                        sp.dma_start(t["h2"][tile], h2[:, j]).then_inc(stored[j], 16)
                        sp.wait_ge(evicted, tile + 2)
                        sp.dma_start(t["h2T"][tile], h2T[:, j]).then_inc(stored[j], 16)
                sp.dma_start(t["h2T"][NT], h2T[:, SL - 1]).then_inc(tail, 16)
                sp.dma_start(t["h2"][NT], h2[:, SL - 1]).then_inc(tail, 16)
                sp.wait_ge(tail, 32)
                for j in range(SL):
                    sp.wait_ge(stored[j], 48 + 48 * (NT // SL))

            @block.gpsimd
            def _(pool):
                nc.gpsimd.memset(t["junk"][:, 0:1], 0.0).then_inc(added, SL)
                nc.gpsimd.memset(t["junk"][:, 1:2], 0.0).then_inc(mixed, SL)
                nc.gpsimd.memset(t["junk"][:, 2:3], 0.0).then_inc(evicted, 1)
                for j in range(SL):
                    nc.gpsimd.memset(t["junk"][:, 3 + j:4 + j], 0.0).then_inc(stored[j], 48)

            @block.scalar
            def _(act):
                def cut_tile(i, j):
                    act.drain()
                    act.wait_ge(mixed, i * SL + j + 1)
                    carry_wait(nc, t, "act")
                    nc.scalar.copy(cat[:, j], catT[:, :, bass.ts(i * SL + j, P)]).then_inc(cut, 1)

                with act.Fori(0, NT // SL) as i:
                    for j in range(SL):
                        cut_tile(i, j)
                    for j in range(SL):
                        tile = i * SL + j
                        act.wait_ge(meansq, tile + 1)
                        nc.scalar.activation(st[:, j, 2:3], st[:, j, 1:2], ACT.Sqrt).then_inc(rooted, 1)
                        act.wait_ge(turned, tile + 1)
                        act.wait_ge(stored[j], i * 48 + 48)
                        nc.scalar.copy(h2T[:, j], ps_t[:].rearrange("p (k n) -> p k n", k=KC)).then_inc(evicted, 1)

            @block.tensor
            def _(pe):
                pe.wait_ge(wo_in, 16)
                with pe.Fori(0, NT // SL) as i:
                    def mix_tile(j):
                        pe.wait_ge(cut, i * SL + j + 1)
                        pe.wait_ge(added, i * SL + j + 1)
                        for k in range(KC):
                            for a in range(2):
                                last = nc.tensor.matmul(mix[j][:, a * BANK:(a + 1) * BANK], cat[:, j, k, :],
                                                        wo[:, k, a * BANK:(a + 1) * BANK], start=(k == 0),
                                                        stop=(k == KC - 1))
                        last.then_inc(mixed, 1)

                    def turn_tile(j):
                        pe.wait_ge(normed, i * SL + j + 1)
                        pe.wait_ge(evicted, i * SL + j + 1)
                        for k in range(KC):
                            last = nc.tensor.transpose(ps_t[:, k * P:(k + 1) * P], h2[:, j, k * P:(k + 1) * P],
                                                       ident[:])
                        last.then_inc(turned, 1)

                    mix_tile(0)
                    mix_tile(1)
                    turn_tile(0)
                    mix_tile(2)
                    turn_tile(1)
                    turn_tile(2)

            @block.vector
            def _(dve):
                dve.wait_ge(vec_in, 7 * 16)
                for c in range(2):
                    nc.vector.scalar_tensor_tensor(out=gain[:, c], in0=gain[:, c], scalar=1.0, in1=g2[:],
                                                   op0=ALU.add, op1=ALU.mult)
                dve.drain()
                with dve.Fori(0, NT // SL) as i:
                    for j in range(SL):
                        tile = i * SL + j
                        cond = (tile + 7) // 8
                        dve.wait_ge(mixed, i * SL + j + 1 + SL)
                        dve.wait_ge(stored[j], i * 48 + 48)
                        nc.vector.tensor_tensor(x1[:, j], mix[j][:], gate[:, cond], ALU.mult)
                        dve.drain()
                        dve.wait_ge(x_in[j], i * 16 + 16)
                        nc.vector.tensor_tensor(x1[:, j], x1[:, j], xt[:, j], ALU.add).then_inc(added, 1)
                        dve.drain()
                        nc.vector.tensor_tensor_reduce(out=h2[:, j], in0=x1[:, j], in1=x1[:, j], scale=1.0,
                                                       scalar=0.0, op0=ALU.mult, op1=ALU.add,
                                                       accum_out=st[:, j, 0:1])
                        dve.drain()
                        nc.vector.tensor_scalar(st[:, j, 1:2], st[:, j, 0:1], 1.0 / D, EPS, ALU.mult,
                                                ALU.add).then_inc(meansq, 1)
                        dve.wait_ge(rooted, tile + 1)
                        nc.vector.reciprocal(st[:, j, 3:4], st[:, j, 2:3])
                        dve.drain()
                        nc.vector.scalar_tensor_tensor(out=h2[:, j], in0=x1[:, j], scalar=st[:, j, 3:4],
                                                       in1=gain[:, cond], op0=ALU.mult, op1=ALU.mult)
                        dve.drain()
                        nc.vector.tensor_tensor(h2[:, j], h2[:, j], shift[:, cond], ALU.add).then_inc(normed, 1)


def peer_stage(nc, ctx, t, ident, started):
    RING = 8
    GROUP = 4
    DIAG = 4
    UNIT = TOPK
    with ExitStack() as own:
        def sb(name, shape, dt=F32):
            return own.enter_context(nc.sbuf_tensor(name, shape, dt))

        def psum(name, shape):
            return own.enter_context(nc.psum_tensor(name, shape, F32))

        def sem(name):
            return ctx.enter_context(nc.semaphore(name))

        wq = sb("wq", [P, KC, PH * 2 * P])
        keys = sb("keys", [P, 2, KEYS])
        urow, vrow = sb("urow", [P, RING, D]), sb("vrow", [P, RING, D])
        h2, h2T, x1, yt = sb("p_h2", [P, D]), sb("p_h2T", [P, KC, P]), sb("p_x1", [P, D]), sb("p_y", [P, D])
        gate, gfin = sb("p_gate", [P, 2, D]), sb("p_gfin", [P, D])
        qs = sb("qs", [P, 2, P])
        sc = sb("sc", [P, 2, KEYS])
        sc2 = sb("sc2", [P, 2, KEYS])
        val, ind = sb("val", [P, 2, TOPK]), sb("ind", [P, 2, TOPK], U32)
        cand, cand2 = sb("cand", [P, TOPK * TOPK]), sb("cand2", [P, TOPK * TOPK])
        best, pos = sb("best", [P, TOPK]), sb("pos", [P, TOPK], U32)
        where = sb("where", [P, 2, TOPK], U32)
        onehot = sb("onehot", [P, 2 * TOPK, TOPK])
        picked = sb("picked", [P, 2, TOPK])
        iota = sb("iota", [P, TOPK])
        expert = sb("expert", [P, 2, TOPK], U32)
        low = sb("neg_best", [P, 1])
        ex, z, rz = sb("ex", [P, TOPK]), sb("z", [P, 1]), sb("rz", [P, 1])
        dot, gelu, wt = sb("dot", [P, TOPK]), sb("gelu", [P, TOPK]), sb("wt", [P, TOPK])
        diag = sb("diag", [P, DIAG, P])
        st = sb("p_st", [P, 4])
        acc, ps_q, ps_s = psum("acc", [P, 2 * BANK]), psum("ps_q", [P, 2, P]), psum("ps_s", [P, 2, KEYS])

        fixed_in = sem("fixed_in")
        h2_in, h2T_in, x1_in = sem("p_h2_in"), sem("p_h2T_in"), sem("p_x1_in")
        u_in = [sem(f"u_in{s}") for s in range(RING)]
        v_in = [sem(f"v_in{s}") for s in range(RING)]
        q_done, q_copied, s_done, s_copied = sem("q_done"), sem("q_copied"), sem("s_done"), sem("s_copied")
        chosen, softened = sem("chosen"), sem("softened")
        dotted, gelued, weighed = sem("dotted"), sem("gelued"), sem("weighed")
        diagonal, summed = sem("diagonal"), sem("summed")
        acc_read, p_meansq, p_rooted, y_ready, y_out = (sem("acc_read"), sem("p_meansq"), sem("p_rooted"),
                                                       sem("y_ready"), sem("y_out"))
        U_T = PH * UNIT

        with nc.Block() as block:
            @block.sync
            def _(sp):
                sp.dma_start(h2T[:], t["h2T"][0]).then_inc(h2T_in, 16)
                sp.dma_start(wq[:], t["wq"]).then_inc(fixed_in, 16)
                sp.dma_start(keys[:], t["keys"]).then_inc(fixed_in, 16)
                sp.dma_start(h2[:], t["h2"][0]).then_inc(h2_in, 16)
                for c in range(2):
                    sp.dma_start(gate[:, c], mod_vector(t, c, 5)).then_inc(fixed_in, 16)
                sp.dma_start(gfin[:], t["g_final"].partition_broadcast(P)).then_inc(fixed_in, 16)
                with sp.Fori(0, NT) as i:
                    sp.wait_ge(acc_read, i + 1)
                    sp.dma_start(x1[:], t["x1"][i]).then_inc(x1_in, 16)
                    sp.wait_ge(q_done, i * PH + PH)
                    sp.dma_start(h2T[:], t["h2T"][i + 1]).then_inc(h2T_in, 16)
                    sp.wait_ge(dotted, i * U_T + (U_T + RING))
                    sp.dma_start(h2[:], t["h2"][i + 1]).then_inc(h2_in, 16)
                    sp.wait_ge(y_ready, i + 1)
                    sp.dma_start(t["y"][i], yt[:]).then_inc(y_out, 16)
                sp.wait_ge(y_out, 16 + 16 * NT)
                sp.wait_ge(h2T_in, 16 * (NT + 1))
                sp.wait_ge(h2_in, 16 * (NT + 1))

            @block.gpsimd
            def _(pool):
                nc.gpsimd.iota(iota[:], pattern=[[1, TOPK]], base=0, channel_multiplier=0,
                               allow_small_or_imprecise_dtypes=True)
                nc.gpsimd.memset(t["junk"][:, 0:1], 0.0).then_inc(dotted, RING)
                nc.gpsimd.memset(t["junk"][:, 1:2], 0.0).then_inc(summed, RING)
                pool.drain()
                nc.gpsimd.memset(t["junk"][:, 2:3], 0.0).then_inc(y_out, 16)
                nc.gpsimd.memset(t["junk"][:, 3:4], 0.0).then_inc(acc_read, 1)
                with pool.Fori(0, NT) as i:
                    for h in range(PH):
                        for table, rows, landed, used in ((t["u"], urow, u_in, dotted), (t["v"], vrow, v_in, summed)):
                            for k in range(UNIT):
                                if k % GROUP == 0:
                                    pool.drain()
                                    pool.wait_ge(chosen, i * PH + (h + 1))
                                    pool.wait_ge(used, i * U_T + (h * UNIT + k + GROUP))
                                    carry_wait(nc, t, "pool")
                                nc.gpsimd.indirect_dma_start(
                                    out=rows[:, k % RING, :], out_offset=None, in_=table,
                                    in_offset=bass.IndirectOffsetOnAxis(ap=expert[:, h % 2, k:k + 1], axis=0),
                                ).then_inc(landed[k % RING], 16)

            @block.tensor
            def _(pe):
                def query(i, h):
                    if h in (0, PH):
                        pe.wait_ge(h2T_in, i * 16 + (16 if h == 0 else 32))
                    c = h % PH
                    for half in range(2):
                        for k in range(KC):
                            last = nc.tensor.matmul(ps_q[:, half, :], wq[:, k, (2 * c + half) * P:(2 * c + half + 1) * P],
                                                    h2T[:, k, :], start=(k == 0), stop=(k == KC - 1))
                    last.then_inc(q_done, 1)
                    pe.wait_ge(q_copied, i * PH + (h + 1))
                    if not isinstance(i, int):
                        pe.wait_ge(s_copied, i * PH + h)
                    for half in range(2):
                        last = nc.tensor.matmul(ps_s[:, half, :], qs[:, half, :], keys[:, half, :], start=True, stop=True)
                    last.then_inc(s_done, 1)

                pe.wait_ge(fixed_in, 5 * 16)
                query(0, 0)
                with pe.Fori(0, NT) as i:
                    for h in range(PH):
                        query(i, h + 1)
                        if h == 0:
                            pe.wait_ge(acc_read, i + 1)
                        for k in range(UNIT):
                            pe.wait_ge(v_in[k % RING], i * (16 * PH * UNIT // RING)
                                       + 16 * (h * (UNIT // RING) + k // RING + 1))
                            pe.wait_ge(diagonal, i * U_T + (h * UNIT + k + 1))
                            for a in range(2):
                                last = nc.tensor.matmul(acc[:, a * BANK:(a + 1) * BANK], diag[:, k % DIAG, :],
                                                        vrow[:, k % RING, a * BANK:(a + 1) * BANK],
                                                        start=(h == 0 and k == 0),
                                                        stop=(h == PH - 1 and k == UNIT - 1))
                            last.then_inc(summed, 1)

            @block.scalar
            def _(act):
                def query(i, h):
                    act.wait_ge(q_done, i * PH + (h + 1))
                    nc.scalar.copy(qs[:], ps_q[:]).then_inc(q_copied, 1)
                    act.wait_ge(s_done, i * PH + (h + 1))
                    if h or not isinstance(i, int):
                        act.wait_ge(chosen, i * PH + h)
                    nc.scalar.copy(sc[:], ps_s[:]).then_inc(s_copied, 1)

                def soften(i, h):
                    act.wait_ge(chosen, i * PH + (h + 1))
                    nc.scalar.activation(ex[:], best[:], ACT.Exp, bias=low[:], accum_out=z[:]).then_inc(softened, 1)

                query(0, 0)
                soften(0, 0)
                with act.Fori(0, NT) as i:
                    for h in range(PH):
                        query(i, h + 1)
                        act.wait_ge(dotted, i * U_T + ((h + 1) * UNIT + RING))
                        nc.scalar.activation(gelu[:], dot[:], ACT.Gelu).then_inc(gelued, 1)
                        act.wait_ge(weighed, i * PH + (h + 1))
                        for k in range(UNIT):
                            act.wait_ge(summed, i * U_T + (h * UNIT + k + 1 + RING - DIAG))
                            nc.scalar.activation(diag[:, k % DIAG, :], ident[:], ACT.Copy, scale=wt[:, k:k + 1])\
                                .then_inc(diagonal, 1)
                        soften(i, h + 1)
                    act.wait_ge(p_meansq, i + 1)
                    nc.scalar.activation(st[:, 2:3], st[:, 1:2], ACT.Sqrt).then_inc(p_rooted, 1)

            @block.vector
            def _(dve):
                def choose(i, h):
                    if not isinstance(i, int):
                        dve.drain()
                        dve.wait_ge(summed, i * U_T + ((h - 1) * UNIT + RING))
                    dve.wait_ge(s_copied, i * PH + (h + 1))
                    carry_wait(nc, t, "dve")
                    nc.vector.max(val[:, 0, 0:8], sc[:, 0])
                    nc.vector.max(val[:, 1, 0:8], sc[:, 1])
                    dve.drain()
                    for s in range(2):
                        nc.vector.max_index(ind[:, s, 0:8], val[:, s, 0:8], sc[:, s])
                        nc.vector.match_replace(sc2[:, s], val[:, s, 0:8], sc[:, s], DROPPED)
                    dve.drain()
                    nc.vector.max(val[:, 0, 8:16], sc2[:, 0])
                    nc.vector.max(val[:, 1, 8:16], sc2[:, 1])
                    dve.drain()
                    for s in range(2):
                        nc.vector.max_index(ind[:, s, 8:16], val[:, s, 8:16], sc2[:, s])
                    nc.vector.tensor_tensor(cand[:].rearrange("p (a b) -> p a b", a=TOPK),
                                            val[:, 0, :].unsqueeze(2).to_broadcast([P, TOPK, TOPK]),
                                            val[:, 1, :].unsqueeze(1).to_broadcast([P, TOPK, TOPK]), ALU.add)
                    dve.drain()
                    if not (isinstance(i, int) and h == 0):
                        dve.wait_ge(softened, i * PH + h)
                        carry_wait(nc, t, "dve")
                    nc.vector.max(best[:, 0:8], cand[:])
                    dve.drain()
                    nc.vector.max_index(pos[:, 0:8], best[:, 0:8], cand[:])
                    nc.vector.match_replace(cand2[:], best[:, 0:8], cand[:], DROPPED)
                    dve.drain()
                    nc.vector.max(best[:, 8:16], cand2[:])
                    dve.drain()
                    nc.vector.max_index(pos[:, 8:16], best[:, 8:16], cand2[:])
                    nc.vector.tensor_scalar(low[:], best[:, 0:1], -1.0, None, ALU.mult)
                    dve.drain()
                    nc.vector.tensor_scalar(where[:, 0], pos[:], 4, None, ALU.logical_shift_right)
                    nc.vector.tensor_scalar(where[:, 1], pos[:], TOPK - 1, None, ALU.bitwise_and)
                    dve.drain()
                    flat = where[:].rearrange("p s k -> p (s k)")
                    nc.vector.tensor_tensor(onehot[:], iota[:].unsqueeze(1).to_broadcast([P, 2 * TOPK, TOPK]),
                                            flat.unsqueeze(2).to_broadcast([P, 2 * TOPK, TOPK]), ALU.is_equal)
                    dve.drain()
                    by_side = onehot[:].rearrange("p (s k) j -> p s k j", s=2)
                    nc.vector.tensor_tensor(by_side, by_side,
                                            ind[:].unsqueeze(2).to_broadcast([P, 2, TOPK, TOPK]), ALU.mult)
                    dve.drain()
                    nc.vector.tensor_reduce(picked[:].rearrange("p s k -> p (s k)"), onehot[:], X, ALU.add)
                    dve.drain()
                    nc.vector.scalar_tensor_tensor(out=expert[:, h % 2, :], in0=picked[:, 0], scalar=float(KEYS),
                                                   in1=picked[:, 1], op0=ALU.mult, op1=ALU.add).then_inc(chosen, 1)

                dve.wait_ge(y_out, 16)
                choose(0, 0)
                dve.wait_ge(fixed_in, 5 * 16)
                with dve.Fori(0, NT) as i:
                    for h in range(PH):
                        if h == 0:
                            dve.wait_ge(h2_in, i * 16 + 16)
                        for k in range(UNIT):
                            dve.wait_ge(u_in[k % RING], i * (16 * PH * UNIT // RING)
                                        + 16 * (h * (UNIT // RING) + k // RING + 1))
                            nc.vector.tensor_tensor_reduce(out=urow[:, k % RING, :], in0=urow[:, k % RING, :],
                                                           in1=h2[:], scale=1.0, scalar=0.0, op0=ALU.mult,
                                                           op1=ALU.add, accum_out=dot[:, k:k + 1])\
                                .then_inc(dotted, 1)
                        dve.wait_ge(softened, i * PH + (h + 1))
                        nc.vector.reciprocal(rz[:], z[:])
                        dve.drain()
                        dve.wait_ge(gelued, i * PH + (h + 1))
                        nc.vector.scalar_tensor_tensor(out=wt[:], in0=gelu[:], scalar=rz[:], in1=ex[:],
                                                       op0=ALU.mult, op1=ALU.mult).then_inc(weighed, 1)
                        choose(i, h + 1)
                    dve.wait_ge(summed, i * U_T + (U_T + RING))
                    dve.wait_ge(y_out, i * 16 + 16)
                    nc.vector.tensor_tensor(yt[:], acc[:], gate[:, (i + 7) // 8], ALU.mult)
                    dve.drain()
                    dve.wait_ge(x1_in, i * 16 + 16)
                    nc.vector.tensor_tensor(yt[:], yt[:], x1[:], ALU.add).then_inc(acc_read, 1)
                    dve.drain()
                    nc.vector.tensor_tensor_reduce(out=onehot[:].rearrange("p a b -> p (a b)")[:, 0:BANK],
                                                   in0=yt[:, 0:BANK], in1=yt[:, 0:BANK], scale=1.0, scalar=0.0,
                                                   op0=ALU.mult, op1=ALU.add, accum_out=st[:, 0:1])
                    dve.drain()
                    nc.vector.tensor_tensor_reduce(out=onehot[:].rearrange("p a b -> p (a b)")[:, 0:BANK],
                                                   in0=yt[:, BANK:D], in1=yt[:, BANK:D], scale=1.0,
                                                   scalar=st[:, 0:1], op0=ALU.mult, op1=ALU.add,
                                                   accum_out=st[:, 3:4])
                    dve.drain()
                    nc.vector.tensor_scalar(st[:, 1:2], st[:, 3:4], 1.0 / D, EPS, ALU.mult, ALU.add)\
                        .then_inc(p_meansq, 1)
                    dve.wait_ge(p_rooted, i + 1)
                    nc.vector.reciprocal(st[:, 0:1], st[:, 2:3])
                    dve.drain()
                    nc.vector.scalar_tensor_tensor(out=yt[:], in0=yt[:], scalar=st[:, 0:1], in1=gfin[:],
                                                   op0=ALU.mult, op1=ALU.mult).then_inc(y_ready, 1)


def build(nc, t):
    with ExitStack() as ctx:
        def sb(name, shape):
            return ctx.enter_context(nc.sbuf_tensor(name, shape, F32))

        ident = sb("ident", [P, P])
        t["junk"], t["tock"], t["carry"] = sb("junk", [P, 8]), sb("tock", [P, 2]), sb("carry", [P, 3])
        t["ident"] = ident
        started = ctx.enter_context(nc.semaphore("started"))
        modulation_stage(nc, ctx, t, ident, started)
        with ExitStack() as mixers:
            def msb(name, shape):
                return mixers.enter_context(nc.sbuf_tensor(name, shape, F32))

            catT = msb("catT", [P, 2 * HEADS, TOK])
            with ExitStack() as inner:
                hT = inner.enter_context(nc.sbuf_tensor("hT", [P, KC, TOK], F32))
                norm_stage(nc, ctx, t, ident, hT, started)
                neg_u = inner.enter_context(nc.sbuf_tensor("neg_u", [HEADS, 2, TOK], F32))
                decay = inner.enter_context(nc.sbuf_tensor("decay", [HEADS, 2, TOK], F32))
                cols = inner.enter_context(nc.sbuf_tensor("cols", [P, 2, 2, NT, HEADS], F32))
                masks = inner.enter_context(nc.sbuf_tensor("masks", [P, 2, P], F32))
                gates_stage(nc, ctx, t, ident, hT, neg_u, decay, cols, masks)
                mixer_stage(nc, ctx, t, ident, hT, catT, neg_u, decay, cols, masks, started)
            output_stage(nc, ctx, t, ident, catT, started)
        peer_stage(nc, ctx, t, ident, started)


def layouts(i):
    import numpy as np
    a = {k: np.asarray(v) for k, v in i.items()}
    w_in = a["w_in"][0]
    out = {
        "x": np.concatenate([a["x_prompt"].reshape(1, P, D), a["x_sample"].reshape(NT - 1, P, D)]),
        "cond": np.stack([a["c_ctx"], a["c"][0]]).reshape(2, KC, P).transpose(2, 1, 0),
        "w_ada": a["w_ada"][0].reshape(KC, P, 12, 512).transpose(2, 1, 0, 3),
        "b_ada": np.concatenate([a["b_ada"][0].reshape(48, P)] * 2),
        "g_norm1": a["g_norm1"][0], "g_norm2": a["g_norm2"][0], "g_final": a["g_final"],
        "w_in": w_in[:, :3584].reshape(KC, P, KINDS, HEADS, P)[:, :, [1, 2, 0, 3, 4, 5, 6]].transpose(3, 2, 1, 0, 4),
        "w_gate": w_in[:, 3584:].reshape(KC, P, 16).transpose(1, 0, 2),
        "b_gate": np.stack([a["b_igate"][0], a["b_fgate"][0]]).reshape(4, HEADS).T,
        "m0": a["state_m"][0, 0].T,
        "state": np.concatenate([a["state_C"][0, 0], a["state_n"][0, 0][..., None]], axis=-1),
        "conv": np.concatenate([a["conv_w"][0], a["conv_b"]]).reshape(4, 4, P).transpose(2, 1, 0),
        "g_mlstm": a["g_mlstm"][0].T,
        "w_out": a["w_out"][0].reshape(KC, P, D).transpose(1, 0, 2),
        "wq": a["peer_wq"][0].reshape(KC, P, PH * 2 * P).transpose(1, 0, 2),
        "keys": np.stack([a["peer_k1"][0], a["peer_k2"][0]]).transpose(2, 0, 1),
        "u": a["peer_u"][0], "v": a["peer_v"][0],
    }
    return {k: np.ascontiguousarray(v) for k, v in out.items()}


OUTS = {"y": (NT, P, D), "new_C": (2, HEADS, DH, DH), "new_n": (2, HEADS, DH, 1), "new_m": (HEADS, 2)}
SCRATCH = {"mod": (96, P), "x1": (NT, P, D), "h2": (NT + 1, P, D), "h2T": (NT + 1, P, KC, P)}


def kernel(**inputs):
    import concourse.bacc as bacc
    from concourse.bass_utils import run_bass_kernel_spmd as run

    nc = bacc.Bacc("TRN2", target_bir_lowering=False, num_devices=1)
    arrays = layouts(inputs)
    t = {k: nc.dram_tensor(f"in_{k}", a.shape, F32, kind="ExternalInput").ap() for k, a in arrays.items()}
    t.update({k: nc.dram_tensor(f"out_{k}", s, F32, kind="ExternalOutput").ap() for k, s in OUTS.items()})
    t.update({k: nc.dram_tensor(f"scratch_{k}", s, F32).ap() for k, s in SCRATCH.items()})
    build(nc, t)
    r = run(nc, [{f"in_{k}": a for k, a in arrays.items()}], core_ids=[0]).results[0]
    y = r["out_y"]
    return (y[0].reshape(1, P, D), y[1:].reshape(1, (NT - 1) * P, D),
            r["out_new_C"].reshape(1, 1, 2, HEADS, DH, DH), r["out_new_n"].reshape(1, 1, 2, HEADS, DH),
            r["out_new_m"].T.reshape(1, 1, 2, HEADS))
```

```python
from contextlib import ExitStack

import concourse.bass as bass
from concourse import mybir

ALU = mybir.AluOpType
ACT = mybir.ActivationFunctionType
F32 = mybir.dt.float32
U32 = mybir.dt.uint32
X = mybir.AxisListType.X

P = 128
D = 1024
KC = D // P
NT = 9
TOK = NT * P
BANK = 512
HEADS = 4
DH = 128
GRID = 64
PH = 8
TOPK = 16
KEYS = 128
EPS = 1e-6
LOW = -1.0e30
DROPPED = -3.0e38
KINDS = 7
CG, XG, BG, Q, K, V, OG = range(KINDS)
SPANS = [(0, 512), (512, 1024), (1024, TOK)]


def carry_wait(nc, t, engine):
    spot = t["carry"]
    if engine == "act":
        nc.scalar.copy(spot[:, 0:1], t["ident"][:, 0:1])
    elif engine == "pool":
        return nc.gpsimd.tensor_tensor(spot[:, 1:2], t["ident"][:, 0:1], t["ident"][:, 0:1], ALU.add)
    else:
        nc.vector.memset(spot[:, 2:3], 0.0)


def modulation_stage(nc, ctx, t, ident, hT, started):
    PIECES, SLOTS = 12, 4
    FIRST = 2 * D // BANK
    HS = 2
    with ExitStack() as own:
        def sb(name, shape):
            return own.enter_context(nc.sbuf_tensor(name, shape, F32))

        def sem(name):
            return ctx.enter_context(nc.semaphore(name))

        wada = sb("wada", [P, SLOTS, KC, BANK])
        cond, silu = sb("cond", [P, KC, 2]), sb("silu", [P, KC, 2])
        mod = sb("mod", [2, 6 * D])
        xt, ht = sb("xt", [P, SLOTS, D]), sb("ht", [P, HS, D])
        st = sb("st", [P, SLOTS, 4])
        gain, shift, g1 = sb("gain", [P, 2, D]), sb("shift", [P, 2, D]), sb("g1", [P, D])
        ps_mod = [own.enter_context(nc.psum_tensor(f"ps_mod{j}", [P, BANK], F32)) for j in range(SLOTS)]
        ps = [own.enter_context(nc.psum_tensor(f"psn{j}", [P, 2 * BANK], F32)) for j in range(HS)]
        cond_in, bias_in, g1_in, vec_in = sem("cond_in"), sem("bias_in"), sem("g1_in"), sem("vec_in")
        piece_in = [sem(f"piece_in{j}") for j in range(SLOTS)]
        x_in = [sem(f"x_in{j}") for j in range(SLOTS)]
        piece_used, biased, silu_done = sem("piece_used"), sem("biased"), sem("silu_done")
        first_out, rest_out = sem("first_mod_out"), sem("rest_mod_out")
        meansq, rooted, normed = sem("meansq"), sem("rooted"), sem("normed")
        turned, evicted = sem("turned"), sem("evicted")

        with nc.Block() as block:
            @block.sync
            def _(sp):
                sp.dma_start(cond[:], t["cond"]).then_inc(cond_in, 16)
                sp.dma_start(mod[:], t["b_ada"].partition_broadcast(2)).then_inc(bias_in, 16)
                for j in range(FIRST):
                    sp.dma_start(wada[:, j], t["w_ada"][j]).then_inc(piece_in[j], 16)
                sp.dma_start(g1[:], t["g_norm1"].partition_broadcast(P)).then_inc(g1_in, 16)

                def load_x(i, j):
                    sp.wait_ge(normed, i * SLOTS + (j + 1))
                    sp.dma_start(xt[:, j], t["x"][i * SLOTS + j]).then_inc(x_in[j], 16)

                with sp.Fori(0, PIECES // SLOTS - 1) as i:
                    for j in range(SLOTS):
                        sp.wait_ge(piece_used, i * SLOTS + (j + 1))
                        sp.dma_start(wada[:, j], t["w_ada"][i * SLOTS + (j + FIRST)]).then_inc(piece_in[j], 16)
                        load_x(i, j)
                load_x(2, 0)
                sp.wait_ge(biased, PIECES)
                sp.dma_start(t["mod"][:, 2 * D:], mod[:, 2 * D:]).then_inc(rest_out, 16)
                sp.wait_ge(rest_out, 16)

            @block.gpsimd
            def _(pool):
                nc.gpsimd.memset(t["junk"][:, 0:1], 0.0).then_inc(normed, SLOTS)
                nc.gpsimd.memset(t["junk"][:, 1:2], 0.0).then_inc(turned, HS)
                nc.gpsimd.memset(t["junk"][:, 2:3], 0.0).then_inc(evicted, HS)
                nc.gpsimd.memset(ident[:], 1.0)
                pool.drain()
                nc.gpsimd.affine_select(out=ident[:], in_=ident[:], compare_op=ALU.is_equal, fill=0.0,
                                        base=0, pattern=[[-1, P]], channel_multiplier=1).then_inc(started, 1)

            @block.scalar
            def _(act):
                act.wait_ge(cond_in, 16)
                nc.scalar.activation(silu[:], cond[:], ACT.Silu).then_inc(silu_done, 1)
                act.wait_ge(biased, FIRST)
                act.dma_start(t["mod"][:, 0:2 * D], mod[:, 0:2 * D]).then_inc(first_out, 16)
                act.wait_ge(first_out, 16)
                for c in range(2):
                    act.dma_start(shift[:, c], mod_vector(t, c, 0)).then_inc(vec_in, 16)
                    act.dma_start(gain[:, c], mod_vector(t, c, 1)).then_inc(vec_in, 16)
                act.wait_ge(started, 1)

                def root_and_evict(i, j):
                    tile = i * SLOTS + j
                    act.wait_ge(meansq, tile + 1)
                    nc.scalar.activation(st[:, j, 2:3], st[:, j, 1:2], ACT.Sqrt).then_inc(rooted, 1)
                    act.drain()
                    act.wait_ge(turned, tile + (1 + HS))
                    carry_wait(nc, t, "act")
                    nc.scalar.copy(hT[:, :, bass.ts(tile, P)],
                                   ps[j % HS][:].rearrange("p (k n) -> p k n", k=KC)).then_inc(evicted, 1)

                with act.Fori(0, NT // SLOTS) as i:
                    for j in range(SLOTS):
                        root_and_evict(i, j)
                root_and_evict(2, 0)

            @block.tensor
            def _(pe):
                def multiply(i, j):
                    pe.wait_ge(piece_in[j], i * 16 + 16)
                    if not isinstance(i, int):
                        pe.wait_ge(biased, (i - 1) * SLOTS + (j + 1))
                    for k in range(KC):
                        last = nc.tensor.matmul(ps_mod[j][0:2, :], silu[:, k, :], wada[:, j, k, :], start=(k == 0),
                                                stop=(k == KC - 1))
                    last.then_inc(piece_used, 1)

                def turn(i, j):
                    pe.wait_ge(normed, i * SLOTS + (j + 1 + SLOTS))
                    pe.wait_ge(evicted, i * SLOTS + (j + 1))
                    for k in range(KC):
                        last = nc.tensor.transpose(ps[j % HS][:, k * P:(k + 1) * P],
                                                   ht[:, j % HS, k * P:(k + 1) * P], ident[:])
                    last.then_inc(turned, 1)

                pe.wait_ge(silu_done, 1)
                for j in range(FIRST):
                    multiply(0, j)
                pe.wait_ge(started, 1)
                with pe.Fori(0, NT // SLOTS) as i:
                    for step, j in ((multiply, 0), (multiply, 1), (turn, 0), (multiply, 2), (turn, 1), (turn, 2),
                                    (multiply, 3), (turn, 3)):
                        step(i + 1 if step is multiply else i, j)
                turn(2, 0)

            @block.vector
            def _(dve):
                def bias(i, j):
                    dve.wait_ge(piece_used, i * SLOTS + (j + 1))
                    at = mod[:, j * BANK:(j + 1) * BANK] if isinstance(i, int) else \
                        mod[:, bass.ts(i * SLOTS + j, BANK)]
                    nc.vector.tensor_tensor(at, ps_mod[j][0:2, :], at, ALU.add).then_inc(biased, 1)

                def norm(i, j):
                    tile = i * SLOTS + j
                    s = j % HS
                    c = (tile + 7) // 8
                    dve.wait_ge(x_in[j], i * 16 + 16)
                    dve.wait_ge(turned, tile + 1)
                    nc.vector.tensor_tensor_reduce(out=ht[:, s], in0=xt[:, j], in1=xt[:, j], scale=1.0,
                                                   scalar=0.0, op0=ALU.mult, op1=ALU.add,
                                                   accum_out=st[:, j, 0:1])
                    dve.drain()
                    nc.vector.tensor_scalar(st[:, j, 1:2], st[:, j, 0:1], 1.0 / D, EPS, ALU.mult,
                                            ALU.add).then_inc(meansq, 1)
                    dve.wait_ge(rooted, tile + 1)
                    nc.vector.reciprocal(st[:, j, 3:4], st[:, j, 2:3])
                    dve.drain()
                    nc.vector.scalar_tensor_tensor(out=ht[:, s], in0=xt[:, j], scalar=st[:, j, 3:4],
                                                   in1=gain[:, c], op0=ALU.mult, op1=ALU.mult)
                    dve.drain()
                    nc.vector.tensor_tensor(ht[:, s], ht[:, s], shift[:, c], ALU.add).then_inc(normed, 1)

                dve.wait_ge(bias_in, 16)
                for j in range(FIRST):
                    bias(0, j)
                dve.wait_ge(g1_in, 16)
                dve.wait_ge(vec_in, 4 * 16)
                for c in range(2):
                    nc.vector.scalar_tensor_tensor(out=gain[:, c], in0=gain[:, c], scalar=1.0, in1=g1[:],
                                                   op0=ALU.add, op1=ALU.mult)
                dve.drain()
                with dve.Fori(0, NT // SLOTS) as i:
                    for j in range(SLOTS):
                        norm(i, j)
                        bias(i + 1, j)
                norm(2, 0)


def mod_vector(t, cond, v):
    return t["mod"][cond, v * D:(v + 1) * D].partition_broadcast(P)


def gates_stage(nc, ctx, t, ident, hT, neg_u, decay, cols, masks):
    with ExitStack() as own:
        wg = own.enter_context(nc.sbuf_tensor("wg", [P, KC, P], F32))
        gb = own.enter_context(nc.sbuf_tensor("gb", [P, 1], F32))
        m0 = own.enter_context(nc.sbuf_tensor("m0", [HEADS, 2], F32))
        keep = own.enter_context(nc.sbuf_tensor("keep", [HEADS, TOK], F32))
        low = own.enter_context(nc.sbuf_tensor("low", [HEADS, TOK], F32))
        gi = own.enter_context(nc.sbuf_tensor("gi", [HEADS, TOK], F32))
        gf = own.enter_context(nc.sbuf_tensor("gf", [HEADS, TOK], F32))
        lg = own.enter_context(nc.sbuf_tensor("lg", [HEADS, TOK], F32))
        bsum = own.enter_context(nc.sbuf_tensor("bsum", [HEADS, TOK], F32))
        gmb = own.enter_context(nc.sbuf_tensor("gmb", [HEADS, 2, TOK], F32))
        top = own.enter_context(nc.sbuf_tensor("top", [HEADS, TOK], F32))
        em = own.enter_context(nc.sbuf_tensor("em", [HEADS, 2, TOK], F32))
        ends = own.enter_context(nc.sbuf_tensor("ends", [HEADS, 3, NT], F32))
        newm = own.enter_context(nc.sbuf_tensor("newm", [HEADS, 2], F32))
        ps = own.enter_context(nc.psum_tensor("psg", [P, 3 * BANK], F32))
        ps_cols = own.enter_context(nc.psum_tensor("psgc", [P, BANK], F32))
        g_in = ctx.enter_context(nc.semaphore("g_in"))
        g_proj = ctx.enter_context(nc.semaphore("g_proj"))
        g_forget = ctx.enter_context(nc.semaphore("g_forget"))
        g_log = ctx.enter_context(nc.semaphore("g_log"))
        g_args = ctx.enter_context(nc.semaphore("g_args"))
        g_exp = ctx.enter_context(nc.semaphore("g_exp"))
        g_cols = ctx.enter_context(nc.semaphore("g_cols"))
        g_masks = ctx.enter_context(nc.semaphore("g_masks"))
        g_out = ctx.enter_context(nc.semaphore("g_out"))
        chunks = lambda a: a.rearrange("h (c n) -> h c n", c=NT)

        with nc.Block() as block:
            @block.sync
            def _(sp):
                sp.dma_start(wg[:], t["w_gate"]).then_inc(g_in, 16)
                sp.dma_start(gb[:], t["b_gate"]).then_inc(g_in, 16)
                sp.dma_start(m0[:], t["m0"]).then_inc(g_in, 16)
                sp.wait_ge(g_args, 2)
                sp.dma_start(t["new_m"], newm[:]).then_inc(g_out, 16)
                sp.wait_ge(g_out, 16)

            @block.gpsimd
            def _(pool):
                nc.gpsimd.memset(masks[:], 1.0)
                pool.drain()
                nc.gpsimd.affine_select(out=masks[:, 0], in_=masks[:, 0], compare_op=ALU.is_ge, fill=0.0,
                                        base=0, pattern=[[1, P]], channel_multiplier=-1)
                nc.gpsimd.affine_select(out=masks[:, 1], in_=masks[:, 1], compare_op=ALU.is_ge, fill=0.0,
                                        base=0, pattern=[[-1, P]], channel_multiplier=1).then_inc(g_masks, 1)

            @block.tensor
            def _(pe):
                pe.wait_ge(g_in, 48)
                for a, b in SPANS:
                    for k in range(KC):
                        last = nc.tensor.matmul(ps[:, a:b], wg[:, k, :], hT[:, k, a:b], start=(k == 0),
                                                stop=(k == KC - 1))
                last.then_inc(g_proj, 1)
                for d in range(2):
                    pe.wait_ge(g_args, d + 1)
                    pe.wait_ge(g_exp, d + 1)
                    for kind, rows in enumerate((gmb, em)):
                        for c in range(NT):
                            at = ((d * 2 + kind) * NT + c) * HEADS
                            last = nc.tensor.transpose(ps_cols[:, at:at + HEADS],
                                                       rows[:, d, c * P:(c + 1) * P],
                                                       ident[0:HEADS, 0:HEADS])
                last.then_inc(g_cols, 1)

            @block.scalar
            def _(act):
                for d in range(2):
                    act.wait_ge(g_forget, d + 1)
                    nc.scalar.activation(lg[:], gf[:], ACT.Abs)
                    act.drain()
                    nc.scalar.activation(lg[:], lg[:], ACT.Exp, scale=-1.0)
                    act.drain()
                    nc.scalar.activation(lg[:], lg[:], ACT.Ln, bias=1.0).then_inc(g_log, 1)
                    act.wait_ge(g_args, d + 1)
                    nc.scalar.activation(decay[:, d], decay[:, d], ACT.Exp)
                    nc.scalar.activation(em[:, d], em[:, d], ACT.Exp).then_inc(g_exp, 1)
                act.wait_ge(g_cols, 1)
                nc.scalar.copy(cols[:].rearrange("p a b c h -> p (a b c h)"), ps_cols[:, 0:16 * NT])

            @block.vector
            def _(dve):
                nc.vector.memset(keep[:], 1.0)
                nc.vector.memset(low[:], 0.0)
                nc.vector.memset(ends[:], 0.0)
                dve.drain()
                nc.vector.memset(chunks(keep[:])[:, :, 0:1], 0.0)
                nc.vector.memset(chunks(low[:])[:, :, 0:1], LOW)
                dve.wait_ge(g_in, 48)
                dve.drain()
                for d in range(2):
                    run = (lambda a: a) if d == 0 else (lambda a: a[:, ::-1])
                    end = P - 1 if d == 0 else 0
                    dve.wait_ge(g_proj, 1)
                    for out, at in ((gi, 32 * d), (gf, 32 * (2 + d))):
                        nc.vector.tensor_scalar(out[:], ps[at:at + HEADS, 0:TOK], gb[at:at + HEADS, :], None,
                                                ALU.add)
                    dve.drain()
                    nc.vector.memset(ends[:, 2, 0:1], 0.0).then_inc(g_forget, 1)
                    dve.wait_ge(g_log, d + 1)
                    nc.vector.scalar_tensor_tensor(out=gf[:], in0=gf[:], scalar=0.0, in1=lg[:],
                                                   op0=ALU.min, op1=ALU.subtract)
                    dve.drain()
                    nc.vector.tensor_tensor_scan(out=run(bsum[:]), data0=keep[:], data1=run(gf[:]), initial=0.0,
                                                 op0=ALU.mult, op1=ALU.add)
                    dve.drain()
                    nc.vector.tensor_tensor(gmb[:, d], gi[:], bsum[:], ALU.subtract)
                    dve.drain()
                    nc.vector.tensor_tensor_scan(out=run(top[:]), data0=low[:], data1=run(gmb[:, d]), initial=0.0,
                                                 op0=ALU.add, op1=ALU.max)
                    dve.drain()
                    nc.vector.tensor_copy(ends[:, 0], chunks(top[:])[:, :, end])
                    nc.vector.tensor_copy(ends[:, 1], chunks(bsum[:])[:, :, end])
                    first = 1 if d == 0 else NT - 1
                    nc.vector.tensor_copy(ends[:, 2, first:first + 1], m0[:, d:d + 1])
                    dve.drain()
                    nc.vector.scalar_tensor_tensor(out=newm[:, d:d + 1], in0=ends[:, 0, 0:1], scalar=0.0,
                                                   in1=ends[:, 1, 0:1], op0=ALU.max, op1=ALU.add)
                    src = slice(1, NT - 1) if d == 0 else slice(NT - 1, 1, -1)
                    dst = slice(2, NT) if d == 0 else slice(NT - 2, 0, -1)
                    nc.vector.tensor_tensor_scan(out=ends[:, 2, dst], data0=ends[:, 0, src], data1=ends[:, 1, src],
                                                 initial=m0[:, d:d + 1], op0=ALU.max, op1=ALU.add)
                    dve.drain()
                    before = ends[:, 2, :].unsqueeze(2).to_broadcast([HEADS, NT, P])
                    nc.vector.tensor_tensor(chunks(top[:]), chunks(top[:]), before, ALU.max)
                    dve.drain()
                    nc.vector.tensor_scalar(neg_u[:, d], top[:], -1.0, None, ALU.mult)
                    nc.vector.tensor_tensor(chunks(decay[:, d]), before, chunks(top[:]), ALU.subtract)
                    dve.drain()
                    nc.vector.tensor_tensor(em[:, d], neg_u[:, d], bsum[:], ALU.subtract).then_inc(g_args, 1)
                    dve.drain()


JOBS = ["q", "k", "v", "ktok", "vtok", "s", "u0", "a0", "og", "kv0", "cg", "num0", "u1", "a1", "xg", "kv1",
        "bg", "num1", "hT"]
NJ = len(JOBS)
PROJ = {"cg": CG, "xg": XG, "bg": BG, "q": Q, "k": K, "v": V, "og": OG}
IN_REGION = [(NJ + 1) // 2, NJ // 2]


def job_done(h, name):
    return h * NJ + (JOBS.index(name) + 1 + NJ)


def evicted(h, name):
    r, value = region_free(h, name)
    return r, value + 1


def region_free(h, name):
    j = JOBS.index(name)
    return j % 2, h * IN_REGION[j % 2] + (j // 2 + 1)


def mixer_stage(nc, ctx, t, ident, hT, neg_u, decay, cols, masks, started):
    W = DH + 1
    with ExitStack() as own:
        def sb(name, shape):
            return own.enter_context(nc.sbuf_tensor(name, shape, F32))

        def sem(name):
            return ctx.enter_context(nc.semaphore(name))

        w = sb("w", [P, KINDS, KC, P])
        qT, kT, vT, og = (sb(n, [P, TOK]) for n in ("qT", "kT", "vT", "ogT"))
        ktok = sb("ktok", [P, NT, P])
        vtok = sb("vtok", [P, NT, W])
        sT = sb("sT", [P, NT, P])
        seen = sb("seen", [P, NT, P])
        qa = sb("qa", [P, NT, P])
        kw = sb("kw", [P, NT, P])
        states = sb("states", [P, NT, W])
        num = sb("num", [P, NT, W])
        hsum = sb("hsum", [P, NT, P])
        u = sb("u", [P, TOK])
        y = sb("y", [P, TOK])
        dec = sb("dec", [P, NT])
        den = sb("den", [P, 2, NT])
        rows = sb("rows", [HEADS, 2, TOK])
        ones = sb("ones", [HEADS, P])
        new = sb("new", [P, 2, W])
        mixed = sb("mixed_rows", [P, 2, TOK])
        conv = sb("conv", [P, 4, 4])
        gm = sb("gm", [P, HEADS])
        region = [own.enter_context(nc.psum_tensor(f"region{r}", [P, 3 * BANK], F32)) for r in range(2)]

        w_in = [sem(f"w_in{k}") for k in range(KINDS)]
        small_in = sem("small_in")
        jobs_done, free = sem("jobs_done"), [sem("region_free0"), sem("region_free1")]
        masked, exped = sem("masked"), sem("exped")
        weighted, ready = sem("k_weighted"), sem("seen_ready")
        h_ready, rooted = sem("h_ready"), sem("h_rooted")
        meansq, state_in = sem("h_meansq"), [sem("state_in0"), sem("state_in1")]
        new_ready, new_out = sem("new_ready"), [sem("new_out0"), sem("new_out1")]
        combined = sem("combined")
        mixed_out = [sem("conv_out"), sem("mlstm_out")]

        def wait_evicted(eng, h, name):
            r, value = evicted(h, name)
            eng.wait_ge(free[r], value)

        def reg(name):
            return region[JOBS.index(name) % 2]

        def toks(name):
            return reg(name)[:, 0:TOK]

        def tiles(name):
            return reg(name)[:, 0:TOK].rearrange("p (c n) -> p c n", c=NT)

        def wide(name):
            return reg(name)[:].rearrange("p (b n) -> p b n", b=3)[:, :, 0:3 * W].rearrange(
                "p b (c n) -> p b c n", c=3)

        def wide_at(name, c):
            return reg(name)[:, (c // 3) * BANK + (c % 3) * W:(c // 3) * BANK + (c % 3 + 1) * W]

        with nc.Block() as block:
            @block.sync
            def _(sp):
                sp.dma_start(conv[:], t["conv"]).then_inc(small_in, 16)
                sp.dma_start(gm[:], t["g_mlstm"]).then_inc(small_in, 16)
                sp.dma_start(states[:, 1], t["state"][0, 0]).then_inc(state_in[0], 16)

                def store_new(h, d):
                    sp.wait_ge(new_ready, h * 2 + (d + 1))
                    sp.dma_start(t["new_C"][d, h], new[:, d, 0:DH]).then_inc(new_out[d], 16)
                    sp.dma_start(t["new_n"][d, h], new[:, d, DH:W]).then_inc(new_out[d], 16)

                for h in range(HEADS + 1):
                    for name in JOBS:
                        if name in PROJ and h < HEADS:
                            sp.wait_ge(jobs_done, h * NJ + (JOBS.index(name) + 1))
                            sp.dma_start(w[:, PROJ[name]], t["w_in"][h, PROJ[name]]).then_inc(w_in[PROJ[name]], 16)
                        if h == 0:
                            continue
                        if name in ("bg", "hT"):
                            wait_evicted(sp, h - 1, name)
                            g = int(name == "hT")
                            sp.dma_start(t["cat"][:, :, g * HEADS + h - 1, :].rearrange("n p c -> p n c"),
                                         mixed[:, g].rearrange("p (n c) -> p n c", n=NT)).then_inc(mixed_out[g], 16)
                        if name in ("kv0", "kv1"):
                            store_new(h - 1, int(name[-1]))
                        elif name == "num0":
                            sp.wait_ge(jobs_done, job_done(h - 1, "num0"))
                            sp.dma_start(states[:, NT - 1], t["state"][1, h - 1]).then_inc(state_in[1], 16)
                        elif name == "num1" and h < HEADS:
                            sp.wait_ge(jobs_done, job_done(h - 1, "num1"))
                            sp.dma_start(states[:, 1], t["state"][0, h]).then_inc(state_in[0], 16)
                for d in range(2):
                    sp.wait_ge(new_out[d], 32 + 32 * HEADS)
                    sp.wait_ge(mixed_out[d], 16 + 16 * HEADS)

            @block.gpsimd
            def _(pool):
                nc.gpsimd.memset(ones[:], 1.0).then_inc(jobs_done, NJ)
                nc.gpsimd.memset(vtok[:, :, DH:W], 1.0).then_inc(free[0], 1)
                nc.gpsimd.memset(t["junk"][:, 0:1], 1.0).then_inc(free[1], 1)
                for d in range(2):
                    nc.gpsimd.memset(t["junk"][:, 1 + d:2 + d], 1.0).then_inc(new_out[d], 32)
                    nc.gpsimd.memset(t["junk"][:, 3 + d:4 + d], 1.0).then_inc(mixed_out[d], 16)

            @block.tensor
            def _(pe):
                with pe.Fori(0, HEADS) as h:
                    def take(name):
                        r, value = region_free(h, name)
                        pe.wait_ge(free[r], value)

                    def project(name):
                        pe.wait_ge(w_in[PROJ[name]], h * 16 + 16)
                        take(name)
                        for k in range(KC):
                            for a, b in SPANS:
                                last = nc.tensor.matmul(reg(name)[:, a:b], w[:, PROJ[name], k, :], hT[:, k, a:b],
                                                        start=(k == 0), stop=(k == KC - 1))
                        last.then_inc(jobs_done, 1)

                    def turn(name, src):
                        for c in range(NT):
                            last = nc.tensor.transpose(tiles(name)[:, c], src[:, c * P:(c + 1) * P], ident[:])
                        last.then_inc(jobs_done, 1)

                    for name in ("q", "k", "v"):
                        project(name)
                    wait_evicted(pe, h, "q")
                    wait_evicted(pe, h, "k")
                    take("ktok")
                    turn("ktok", kT)
                    wait_evicted(pe, h, "v")
                    take("vtok")
                    turn("vtok", vT)
                    take("s")
                    for c in range(NT):
                        last = nc.tensor.matmul(tiles("s")[:, c], kT[:, c * P:(c + 1) * P], qT[:, c * P:(c + 1) * P],
                                                start=True, stop=True)
                    last.then_inc(jobs_done, 1)

                    def spread_rows(d):
                        pe.wait_ge(masked, h * 2 + (d + 1))
                        for kind, name in enumerate((f"u{d}", f"a{d}")):
                            take(name)
                            for a, b in SPANS:
                                last = nc.tensor.matmul(reg(name)[:, a:b], ones[:], rows[:, kind, a:b],
                                                        start=True, stop=True)
                            last.then_inc(jobs_done, 1)

                    def outer(d):
                        pe.wait_ge(weighted, h * 2 + (d + 1))
                        take(f"kv{d}")
                        for c in range(NT):
                            last = nc.tensor.matmul(wide_at(f"kv{d}", c), kw[:, c, :], vtok[:, c, :],
                                                    start=True, stop=True)
                        last.then_inc(jobs_done, 1)

                    def numerators(d):
                        pe.wait_ge(ready, h * 2 + (d + 1))
                        wait_evicted(pe, h, "vtok")
                        wait_evicted(pe, h, f"kv{d}")
                        take(f"num{d}")
                        for c in range(NT):
                            last = nc.tensor.matmul(wide_at(f"num{d}", c), seen[:, c, :], vtok[:, c, :],
                                                    start=True, stop=(c == 0))
                            if c:
                                last = nc.tensor.matmul(wide_at(f"num{d}", c), qa[:, c, :], states[:, c, :],
                                                        start=False, stop=True)
                        last.then_inc(jobs_done, 1)

                    spread_rows(0)
                    project("og")
                    outer(0)
                    project("cg")
                    numerators(0)
                    spread_rows(1)
                    project("xg")
                    outer(1)
                    project("bg")
                    numerators(1)
                    pe.wait_ge(h_ready, h + 1)
                    take("hT")
                    for c in range(NT):
                        last = nc.tensor.transpose(tiles("hT")[:, c], hsum[:, c, :], ident[:])
                    last.then_inc(jobs_done, 1)

            @block.scalar
            def _(act):
                with act.Fori(0, HEADS) as h:
                    def evict(name, out, src, func=ACT.Copy, scale=1.0):
                        act.wait_ge(jobs_done, job_done(h, name))
                        nc.scalar.activation(out, src, func, scale=scale).then_inc(free[JOBS.index(name) % 2], 1)

                    evict("q", qT[:], toks("q"), scale=float(DH) ** -0.5)
                    evict("k", kT[:], toks("k"))
                    evict("v", vT[:], toks("v"))
                    evict("ktok", ktok[:], tiles("ktok"))
                    evict("vtok", vtok[:, :, 0:DH], tiles("vtok"))
                    evict("s", sT[:], tiles("s"))

                    def exps(d):
                        wait_evicted(act, h, f"u{d}")
                        nc.scalar.activation(seen[:], seen[:], ACT.Exp).then_inc(exped, 1)
                        evict(f"a{d}", qa[:], tiles(f"a{d}"))

                    def copy_num(d):
                        if d:
                            act.wait_ge(combined, h * 2 + 2 + 1)
                        act.wait_ge(jobs_done, job_done(h, f"num{d}"))
                        for b in range(3):
                            last = nc.scalar.copy(num[:, 3 * b:3 * b + 3, :], wide(f"num{d}")[:, b])
                        last.then_inc(free[JOBS.index(f"num{d}") % 2], 1)

                    exps(0)
                    evict("og", og[:], toks("og"), func=ACT.Sigmoid)
                    evict("cg", u[:], toks("cg"))
                    copy_num(0)
                    exps(1)
                    copy_num(1)
                    act.wait_ge(meansq, h + 1)
                    nc.scalar.activation(den[:, 1, :], den[:, 0, :], ACT.Sqrt).then_inc(rooted, 1)

            @block.vector
            def _(dve):
                nc.vector.memset(t["tock"][:, 0:2], 0.0).then_inc(combined, 2)
                dve.wait_ge(small_in, 32)
                with dve.Fori(0, HEADS) as h:
                    def mask_rows(d):
                        if d:
                            dve.wait_ge(jobs_done, job_done(h, "a0"))
                        for kind, src in enumerate((neg_u, decay)):
                            last = nc.vector.tensor_scalar(rows[:, kind], src[:, d], ident[0:HEADS, bass.ds(h, 1)],
                                                           None, ALU.mult)
                        last.then_inc(masked, 1)

                    def arguments(d):
                        dve.wait_ge(jobs_done, job_done(h, f"u{d}"))
                        for c in range(NT):
                            last = nc.vector.tensor_scalar(seen[:, c, :], tiles(f"u{d}")[:, c],
                                                           cols[:, d, 0, c, bass.ds(h, 1)], 0.0, ALU.add, ALU.min)
                        last.then_inc(free[JOBS.index(f"u{d}") % 2], 1)

                    def weights(d):
                        end = P - 1 if d == 0 else 0
                        dve.wait_ge(exped, h * 2 + (d + 1))
                        wait_evicted(dve, h, "ktok")
                        wait_evicted(dve, h, f"a{d}")
                        nc.vector.tensor_copy(dec[:], qa[:, :, end])
                        nc.vector.tensor_tensor(kw[:], ktok[:], seen[:, :, end:end + 1].to_broadcast([P, NT, P]),
                                                ALU.mult).then_inc(weighted, 1)
                        dve.drain()
                        nc.vector.tensor_tensor(qa[:], qa[:], qT[:].rearrange("p (c n) -> p c n", c=NT), ALU.mult)
                        nc.vector.tensor_tensor(seen[:], seen[:],
                                                masks[:, d, :].unsqueeze(1).to_broadcast([P, NT, P]), ALU.mult)
                        dve.drain()
                        nc.vector.tensor_tensor(seen[:], seen[:], sT[:], ALU.mult).then_inc(ready, 1)

                    def chain(d):
                        dve.wait_ge(state_in[d], h * 16 + 16)
                        dve.wait_ge(jobs_done, job_done(h, f"kv{d}"))
                        dve.wait_ge(new_out[d], h * 32 + 32)
                        nc.vector.tensor_copy(new[:, d], wide_at(f"kv{d}", 0)).then_inc(new_ready, 1)
                        order = list(range(1, NT - 1)) if d == 0 else list(range(NT - 1, 1, -1))
                        for c in order:
                            last = nc.vector.scalar_tensor_tensor(out=states[:, c + 1 if d == 0 else c - 1],
                                                           in0=states[:, c], scalar=dec[:, c:c + 1],
                                                           in1=wide_at(f"kv{d}", c), op0=ALU.mult, op1=ALU.add)
                            if c == order[-1]:
                                last.then_inc(free[JOBS.index(f"kv{d}") % 2], 1)
                            dve.drain()

                    def combine(d):
                        wait_evicted(dve, h, f"num{d}")
                        nc.vector.scalar_tensor_tensor(out=den[:, 0, :], in0=num[:, :, DH], scalar=-1.0,
                                                       in1=num[:, :, DH], op0=ALU.mult, op1=ALU.max)
                        dve.drain()
                        nc.vector.tensor_tensor(den[:, 0, :], den[:, 0, :], cols[:, d, 1, :, h], ALU.max)
                        dve.drain()
                        nc.vector.reciprocal(den[:, 1, :], den[:, 0, :])
                        dve.drain()
                        r = den[:, 1, :].unsqueeze(2).to_broadcast([P, NT, P])
                        if d == 0:
                            nc.vector.tensor_tensor(hsum[:], num[:, :, 0:DH], r, ALU.mult).then_inc(combined, 1)
                        else:
                            nc.vector.tensor_tensor(num[:, :, 0:DH], num[:, :, 0:DH], r, ALU.mult)
                            dve.drain()
                            nc.vector.tensor_tensor(hsum[:], hsum[:], num[:, :, 0:DH], ALU.add)\
                                .then_inc(combined, 1)
                        dve.drain()

                    mask_rows(0)
                    arguments(0)
                    weights(0)
                    mask_rows(1)
                    chain(0)
                    combine(0)
                    arguments(1)
                    weights(1)

                    dve.wait_ge(jobs_done, job_done(h, "xg"))
                    nc.vector.tensor_tensor(u[:], toks("xg"), u[:], ALU.mult)\
                        .then_inc(free[JOBS.index("xg") % 2], 1)
                    dve.drain()
                    nc.vector.tensor_scalar(y[:], u[:], conv[:, h, 1:2], conv[:, h, 3:4], ALU.mult, ALU.add)
                    dve.drain()
                    for tap, (to, frm) in ((0, (slice(1, None), slice(0, -1))), (2, (slice(0, -1), slice(1, None)))):
                        for a, b, n in ((0, P, P), (P, TOK, GRID)):
                            yr = y[:, a:b].rearrange("p (r n) -> p r n", n=n)
                            ur = u[:, a:b].rearrange("p (r n) -> p r n", n=n)
                            nc.vector.scalar_tensor_tensor(out=yr[:, :, to], in0=ur[:, :, frm],
                                                           scalar=conv[:, h, tap:tap + 1], in1=yr[:, :, to],
                                                           op0=ALU.mult, op1=ALU.add)
                        dve.drain()
                    chain(1)
                    dve.wait_ge(jobs_done, job_done(h, "bg"))
                    dve.wait_ge(mixed_out[0], h * 16 + 16)
                    nc.vector.tensor_tensor(mixed[:, 0], toks("bg"), y[:], ALU.mult)\
                        .then_inc(free[JOBS.index("bg") % 2], 1)

                    combine(1)
                    nc.vector.tensor_tensor(kw[:], hsum[:], hsum[:], ALU.mult)
                    dve.drain()
                    nc.vector.tensor_reduce(den[:, 1, :], kw[:], X, ALU.add)
                    dve.drain()
                    nc.vector.tensor_scalar(den[:, 0, :], den[:, 1, :], 1.0 / DH, EPS, ALU.mult, ALU.add)\
                        .then_inc(meansq, 1)
                    dve.wait_ge(rooted, h + 1)
                    nc.vector.reciprocal(den[:, 0, :], den[:, 1, :])
                    dve.drain()
                    nc.vector.tensor_tensor(hsum[:], hsum[:], den[:, 0, :].unsqueeze(2).to_broadcast([P, NT, P]),
                                            ALU.mult).then_inc(h_ready, 1)
                    dve.wait_ge(jobs_done, job_done(h, "hT"))
                    dve.wait_ge(mixed_out[1], h * 16 + 16)
                    nc.vector.scalar_tensor_tensor(out=mixed[:, 1], in0=toks("hT"), scalar=gm[:, bass.ds(h, 1)],
                                                   in1=og[:], op0=ALU.mult, op1=ALU.mult)\
                        .then_inc(free[JOBS.index("hT") % 2], 1)


def peer_stage(nc, ctx, t, ident, started):
    RING = 8
    DIAG = 2
    UNIT = TOPK
    GROUP = 2
    GROUPS = UNIT // GROUP
    CHOOSE_AFTER = 1
    TAKE_AFTER = 3
    MIX_UNITS, NEXT_UNIT, RESIDUAL_AFTER, MODULATE_AFTER, TURN_UNIT = (3, 4), 5, 4, 6, 6
    with ExitStack() as own:
        def sb(name, shape, dt=F32):
            return own.enter_context(nc.sbuf_tensor(name, shape, dt))

        def psum(name, shape):
            return own.enter_context(nc.psum_tensor(name, shape, F32))

        def sem(name):
            return ctx.enter_context(nc.semaphore(name))

        wq = sb("wq", [P, KC, PH * 2 * P])
        keys = sb("keys", [P, 2, KEYS])
        uv = sb("uv", [P, RING, 2 * D])
        h2, h2T, x1 = sb("h2", [P, D]), sb("h2T", [P, KC, P]), sb("x1", [P, D])
        next_x, next_h = sb("next_x", [P, D]), sb("next_h", [P, D])
        cat = next_h[:].rearrange("p (k n) -> p k n", k=KC)
        wo = sb("wo", [P, KC, D])
        gate1, gain, shift = sb("gate1", [P, D]), sb("gain2", [P, D]), sb("shift2", [P, D])
        gate2, gfin = sb("gate2", [P, D]), sb("p_gfin", [P, D])
        g2, gate1_c, gain_c, shift_c = uv[:, 0, 0:D], uv[:, 0, D:], uv[:, 1, 0:D], uv[:, 1, D:]
        qs = sb("qs", [P, 2, P])
        sc = qs
        val, ind = sb("val", [P, 2, TOPK]), sb("ind", [P, 2, TOPK], U32)
        work = sb("work", [P, 2 * TOPK * TOPK])
        cand, cand2 = work[:, 0:TOPK * TOPK], work[:, TOPK * TOPK:]
        sc2 = work[:, TOPK * TOPK:].rearrange("p (s k) -> p s k", s=2)
        onehot = work[:].rearrange("p (k j) -> p k j", j=TOPK)
        best, pos = sb("best", [P, TOPK]), sb("pos", [P, TOPK], U32)
        where = sb("where", [P, 2, TOPK], U32)
        picked = sb("picked", [P, 2, TOPK])
        iota = sb("iota", [P, TOPK])
        expert = sb("expert", [P, 2, TOPK], U32)
        low = sb("neg_best", [P, 1])
        ex, z, rz = sb("ex", [P, 2, TOPK]), sb("z", [P, 2]), sb("rz", [P, 2])
        dot, gelu, wt = sb("dot", [P, 2, TOPK]), sb("gelu", [P, 2, TOPK]), sb("wt", [P, 2, TOPK])
        diag = sb("diag", [P, DIAG, P])
        st, next_st = sb("p_st", [P, 4]), sb("next_st", [P, 4])
        acc, ps_q, ps_s = psum("acc", [P, 2 * BANK]), psum("ps_q", [P, 2, P]), psum("ps_s", [P, 2, KEYS])
        mix, ps_t = psum("mix", [P, 2 * BANK]), psum("ps_t", [P, 2 * BANK])

        fixed_in = sem("fixed_in")
        context_in, latent_in, wo_in = sem("context_in"), sem("latent_in"), sem("wo_in")
        x_in, cat_in, gate2_in = sem("next_x_in"), sem("cat_in"), sem("gate2_in")
        mixed, mix_read, next_meansq, next_rooted = sem("mixed"), sem("mix_read"), sem("n_meansq"), sem("n_rooted")
        normed, turned, h2T_ready, handed = sem("h2_ready"), sem("h2_turned"), sem("h2T_ready"), sem("handed")
        rows_in = [sem(f"rows_in{s}") for s in range(RING)]
        q_done, q_copied, s_done, s_copied = sem("q_done"), sem("q_copied"), sem("s_done"), sem("s_copied")
        chosen, softened = sem("chosen"), sem("softened")
        dotted, gelued, weighed = sem("dotted"), sem("gelued"), sem("weighed")
        diagonal, summed = sem("diagonal"), sem("summed")
        acc_read = sem("acc_read")
        p_meansq, p_rooted, y_ready, y_out = sem("p_meansq"), sem("p_rooted"), sem("y_ready"), sem("y_out")
        carried = sem("p_carried")
        U_T = PH * UNIT
        G_T = PH * GROUPS

        with nc.Block() as block:
            @block.sync
            def _(sp):
                sp.dma_start(cat, t["cat"][0]).then_inc(cat_in, 16)
                sp.dma_start(wo[:], t["w_out"]).then_inc(wo_in, 16)
                sp.dma_start(next_x[:], t["x"][0]).then_inc(x_in, 16)
                sp.dma_start(g2, t["g_norm2"].partition_broadcast(P)).then_inc(context_in, 16)
                for vector, v in ((gate1_c, 2), (gain_c, 4), (shift_c, 3)):
                    sp.dma_start(vector, mod_vector(t, 0, v)).then_inc(context_in, 16)
                sp.dma_start(wq[:], t["wq"]).then_inc(fixed_in, 16)
                sp.dma_start(keys[:], t["keys"]).then_inc(fixed_in, 16)
                for vector, v in ((gate1, 2), (gain, 4), (shift, 3)):
                    sp.dma_start(vector[:], mod_vector(t, 1, v)).then_inc(latent_in, 16)
                sp.dma_start(gfin[:], t["g_final"].partition_broadcast(P)).then_inc(latent_in, 16)
                with sp.Fori(0, NT) as i:
                    sp.wait_ge(acc_read, i + 1)
                    sp.dma_start(gate2[:], t["mod"][(i + 7) // 8, 5 * D:6 * D].partition_broadcast(P))\
                        .then_inc(gate2_in, 16)
                    after = (i + 2) * (NT - 1) // NT
                    sp.wait_ge(handed, i + 1)
                    sp.dma_start(next_x[:], t["x"][after]).then_inc(x_in, 16)
                    sp.wait_ge(turned, i + 1)
                    sp.dma_start(cat, t["cat"][after]).then_inc(cat_in, 16)
                    sp.wait_ge(y_ready, i + 1)
                    sp.dma_start(t["y"][i], x1[:]).then_inc(y_out, 16)
                sp.wait_ge(y_out, 16 + 16 * NT)

            @block.gpsimd
            def _(pool):
                nc.gpsimd.iota(iota[:], pattern=[[1, TOPK]], base=0, channel_multiplier=0,
                               allow_small_or_imprecise_dtypes=True)
                nc.gpsimd.memset(t["junk"][:, 0:1], 0.0).then_inc(carried, 1)
                nc.gpsimd.memset(t["junk"][:, 1:2], 0.0).then_inc(summed, RING)
                pool.drain()
                nc.gpsimd.memset(t["junk"][:, 2:3], 0.0).then_inc(y_out, 16)
                nc.gpsimd.memset(t["junk"][:, 3:4], 0.0).then_inc(acc_read, 1)
                with pool.Fori(0, NT) as i:
                    for h in range(PH):
                        for k in range(UNIT):
                            if k % GROUP == 0:
                                pool.wait_ge(chosen, i * PH + (h + 1))
                                pool.wait_ge(carried, i * G_T + (h * GROUPS + k // GROUP + 1))
                                pool.wait_ge(summed, i * U_T + (h * UNIT + k + GROUP))
                                carry_wait(nc, t, "pool").then_inc(carried, 1)
                            nc.gpsimd.indirect_dma_start(
                                out=uv[:, k % RING, :], out_offset=None, in_=t["uv"],
                                in_offset=bass.IndirectOffsetOnAxis(ap=expert[:, h % 2, k:k + 1], axis=0),
                            ).then_inc(rows_in[k % RING], 16)

            @block.tensor
            def _(pe):
                def query(i, h):
                    if h in (0, PH):
                        pe.wait_ge(h2T_ready, i + (1 if h == 0 else 2))
                    c = h % PH
                    for half in range(2):
                        for k in range(KC):
                            last = nc.tensor.matmul(ps_q[:, half, :], wq[:, k, (2 * c + half) * P:(2 * c + half + 1) * P],
                                                    h2T[:, k, :], start=(k == 0), stop=(k == KC - 1))
                    last.then_inc(q_done, 1)
                    pe.wait_ge(q_copied, i * PH + (h + 1))
                    if not isinstance(i, int):
                        pe.wait_ge(s_copied, i * PH + h)
                    for half in range(2):
                        last = nc.tensor.matmul(ps_s[:, half, :], qs[:, half, :], keys[:, half, :], start=True, stop=True)
                    last.then_inc(s_done, 1)

                def mix_half(n, a):
                    pe.wait_ge(cat_in, n * 16 + 16)
                    if not isinstance(n, int):
                        pe.wait_ge(mix_read, n)
                    for k in range(KC):
                        last = nc.tensor.matmul(mix[:, a * BANK:(a + 1) * BANK], cat[:, k, :],
                                                wo[:, k, a * BANK:(a + 1) * BANK], start=(k == 0),
                                                stop=(k == KC - 1))
                    last.then_inc(mixed, 1)

                def turn(n):
                    pe.wait_ge(normed, n + 1)
                    if not isinstance(n, int):
                        pe.wait_ge(h2T_ready, n)
                    for k in range(KC):
                        last = nc.tensor.transpose(ps_t[:, k * P:(k + 1) * P], next_h[:, k * P:(k + 1) * P], ident[:])
                    last.then_inc(turned, 1)

                pe.wait_ge(wo_in, 16)
                mix_half(0, 0)
                mix_half(0, 1)
                turn(0)
                pe.wait_ge(fixed_in, 2 * 16)
                query(0, 0)
                with pe.Fori(0, NT) as i:
                    for h in range(PH):
                        query(i, h + 1)
                        if h in MIX_UNITS:
                            mix_half(i + 1, MIX_UNITS.index(h))
                        if h == 0:
                            pe.wait_ge(acc_read, i + 1)
                        for k in range(UNIT):
                            pe.wait_ge(rows_in[k % RING], i * (16 * PH * UNIT // RING)
                                       + 16 * (h * (UNIT // RING) + k // RING + 1))
                            pe.wait_ge(diagonal, i * U_T + (h * UNIT + k + 1))
                            for a in range(2):
                                last = nc.tensor.matmul(acc[:, a * BANK:(a + 1) * BANK], diag[:, k % DIAG, :],
                                                        uv[:, k % RING, D + a * BANK:D + (a + 1) * BANK],
                                                        start=(h == 0 and k == 0),
                                                        stop=(h == PH - 1 and k == UNIT - 1))
                            last.then_inc(summed, 1)
                        if h == TURN_UNIT:
                            turn(i + 1)

            @block.scalar
            def _(act):
                def query(i, h):
                    act.wait_ge(q_done, i * PH + (h + 1))
                    if h or not isinstance(i, int):
                        act.wait_ge(chosen, i * PH + h)
                    nc.scalar.copy(qs[:], ps_q[:]).then_inc(q_copied, 1)
                    act.wait_ge(s_done, i * PH + (h + 1))
                    nc.scalar.copy(sc[:], ps_s[:]).then_inc(s_copied, 1)

                def soften(i, h):
                    act.wait_ge(chosen, i * PH + (h + 1))
                    nc.scalar.activation(ex[:, h % 2], best[:], ACT.Exp, bias=low[:],
                                         accum_out=z[:, h % 2:h % 2 + 1]).then_inc(softened, 1)

                def root_next(n):
                    act.wait_ge(next_meansq, n + 1)
                    nc.scalar.activation(next_st[:, 2:3], next_st[:, 1:2], ACT.Sqrt).then_inc(next_rooted, 1)

                def evict_h2T(n):
                    act.wait_ge(turned, n + 1)
                    nc.scalar.copy(h2T[:], ps_t[:].rearrange("p (k n) -> p k n", k=KC)).then_inc(h2T_ready, 1)

                root_next(0)
                evict_h2T(0)
                query(0, 0)
                soften(0, 0)
                with act.Fori(0, NT) as i:
                    for h in range(PH):
                        query(i, h + 1)
                        for g in range(GROUPS):
                            ks = slice(g * GROUP, (g + 1) * GROUP)
                            act.wait_ge(dotted, i * G_T + (h * GROUPS + g + 1))
                            nc.scalar.activation(gelu[:, h % 2, ks], dot[:, h % 2, ks], ACT.Gelu).then_inc(gelued, 1)
                            act.wait_ge(weighed, i * G_T + (h * GROUPS + g + 1))
                            for k in range(g * GROUP, (g + 1) * GROUP):
                                act.wait_ge(summed, i * U_T + (h * UNIT + k + 1 + RING - DIAG))
                                nc.scalar.activation(diag[:, k % DIAG, :], ident[:], ACT.Copy,
                                                     scale=wt[:, h % 2, k:k + 1]).then_inc(diagonal, 1)
                            if g == CHOOSE_AFTER:
                                soften(i, h + 1)
                            if h == NEXT_UNIT and g == RESIDUAL_AFTER:
                                root_next(i + 1)
                        if h == TURN_UNIT:
                            evict_h2T(i + 1)
                    act.wait_ge(p_meansq, i + 1)
                    nc.scalar.activation(st[:, 2:3], st[:, 1:2], ACT.Sqrt).then_inc(p_rooted, 1)

            @block.vector
            def _(dve):
                def choose(i, h):
                    dve.drain()
                    dve.wait_ge(s_copied, i * PH + (h + 1))
                    carry_wait(nc, t, "dve")
                    nc.vector.max(val[:, 0, 0:8], sc[:, 0])
                    nc.vector.max(val[:, 1, 0:8], sc[:, 1])
                    dve.drain()
                    for s in range(2):
                        nc.vector.max_index(ind[:, s, 0:8], val[:, s, 0:8], sc[:, s])
                        nc.vector.match_replace(sc2[:, s, :], val[:, s, 0:8], sc[:, s], DROPPED)
                    dve.drain()
                    nc.vector.max(val[:, 0, 8:16], sc2[:, 0, :])
                    nc.vector.max(val[:, 1, 8:16], sc2[:, 1, :])
                    dve.drain()
                    for s in range(2):
                        nc.vector.max_index(ind[:, s, 8:16], val[:, s, 8:16], sc2[:, s, :])
                    nc.vector.tensor_tensor(cand.rearrange("p (a b) -> p a b", a=TOPK),
                                            val[:, 0, :].unsqueeze(2).to_broadcast([P, TOPK, TOPK]),
                                            val[:, 1, :].unsqueeze(1).to_broadcast([P, TOPK, TOPK]), ALU.add)
                    dve.drain()
                    if not (isinstance(i, int) and h == 0):
                        dve.wait_ge(softened, i * PH + h)
                        carry_wait(nc, t, "dve")
                    nc.vector.max(best[:, 0:8], cand)
                    dve.drain()
                    nc.vector.max_index(pos[:, 0:8], best[:, 0:8], cand)
                    nc.vector.match_replace(cand2, best[:, 0:8], cand, DROPPED)
                    dve.drain()
                    nc.vector.max(best[:, 8:16], cand2)
                    dve.drain()
                    nc.vector.max_index(pos[:, 8:16], best[:, 8:16], cand2)
                    nc.vector.tensor_scalar(low[:], best[:, 0:1], -1.0, None, ALU.mult)
                    dve.drain()
                    nc.vector.tensor_scalar(where[:, 0], pos[:], 4, None, ALU.logical_shift_right)
                    nc.vector.tensor_scalar(where[:, 1], pos[:], TOPK - 1, None, ALU.bitwise_and)
                    dve.drain()
                    flat = where[:].rearrange("p s k -> p (s k)")
                    nc.vector.tensor_tensor(onehot, iota[:].unsqueeze(1).to_broadcast([P, 2 * TOPK, TOPK]),
                                            flat.unsqueeze(2).to_broadcast([P, 2 * TOPK, TOPK]), ALU.is_equal)
                    dve.drain()
                    by_side = onehot.rearrange("p (s k) j -> p s k j", s=2)
                    nc.vector.tensor_tensor(by_side, by_side,
                                            ind[:].unsqueeze(2).to_broadcast([P, 2, TOPK, TOPK]), ALU.mult)
                    dve.drain()
                    nc.vector.tensor_reduce(picked[:].rearrange("p s k -> p (s k)"), onehot, X, ALU.add)
                    dve.drain()
                    nc.vector.scalar_tensor_tensor(out=expert[:, h % 2, :], in0=picked[:, 0], scalar=float(KEYS),
                                                   in1=picked[:, 1], op0=ALU.mult, op1=ALU.add).then_inc(chosen, 1)

                def weigh(i, h, g):
                    ks = slice(g * GROUP, (g + 1) * GROUP)
                    if g == 0:
                        dve.wait_ge(softened, i * PH + (h + 1))
                        nc.vector.reciprocal(rz[:, h % 2:h % 2 + 1], z[:, h % 2:h % 2 + 1])
                        dve.drain()
                    dve.wait_ge(gelued, i * G_T + (h * GROUPS + g + 1))
                    nc.vector.scalar_tensor_tensor(out=wt[:, h % 2, ks], in0=gelu[:, h % 2, ks],
                                                   scalar=rz[:, h % 2:h % 2 + 1], in1=ex[:, h % 2, ks],
                                                   op0=ALU.mult, op1=ALU.mult).then_inc(weighed, 1)

                def residual(n, gate1):
                    dve.wait_ge(mixed, n * 2 + 2)
                    nc.vector.tensor_tensor(next_h[:], mix[:], gate1, ALU.mult).then_inc(mix_read, 1)
                    dve.drain()
                    dve.wait_ge(x_in, n * 16 + 16)
                    nc.vector.tensor_tensor(next_x[:], next_x[:], next_h[:], ALU.add)
                    dve.drain()
                    nc.vector.tensor_tensor_reduce(out=next_h[:], in0=next_x[:], in1=next_x[:], scale=1.0, scalar=0.0,
                                                   op0=ALU.mult, op1=ALU.add, accum_out=next_st[:, 0:1])
                    dve.drain()
                    nc.vector.tensor_scalar(next_st[:, 1:2], next_st[:, 0:1], 1.0 / D, EPS, ALU.mult, ALU.add)\
                        .then_inc(next_meansq, 1)

                def modulate(n, gain, shift):
                    dve.wait_ge(next_rooted, n + 1)
                    nc.vector.reciprocal(next_st[:, 3:4], next_st[:, 2:3])
                    dve.drain()
                    nc.vector.scalar_tensor_tensor(out=next_h[:], in0=next_x[:], scalar=next_st[:, 3:4], in1=gain,
                                                   op0=ALU.mult, op1=ALU.mult)
                    dve.drain()
                    nc.vector.tensor_tensor(next_h[:], next_h[:], shift, ALU.add).then_inc(normed, 1)

                dve.wait_ge(y_out, 16)
                dve.wait_ge(context_in, 4 * 16)
                nc.vector.scalar_tensor_tensor(out=gain_c, in0=gain_c, scalar=1.0, in1=g2, op0=ALU.add, op1=ALU.mult)
                residual(0, gate1_c)
                modulate(0, gain_c, shift_c)
                dve.wait_ge(latent_in, 4 * 16)
                nc.vector.scalar_tensor_tensor(out=gain[:], in0=gain[:], scalar=1.0, in1=g2, op0=ALU.add, op1=ALU.mult)
                choose(0, 0)
                with dve.Fori(0, NT) as i:
                    nc.vector.tensor_copy(h2[:], next_h[:])
                    dve.drain()
                    for h in range(PH):
                        for g in range(GROUPS):
                            for k in range(g * GROUP, (g + 1) * GROUP):
                                dve.wait_ge(rows_in[k % RING], i * (16 * PH * UNIT // RING)
                                            + 16 * (h * (UNIT // RING) + k // RING + 1))
                                last = nc.vector.tensor_tensor_reduce(
                                    out=uv[:, k % RING, 0:D], in0=uv[:, k % RING, 0:D], in1=h2[:], scale=1.0,
                                    scalar=0.0, op0=ALU.mult, op1=ALU.add, accum_out=dot[:, h % 2, k:k + 1])
                            last.then_inc(dotted, 1)
                            weigh(i, h, g)
                            if g == CHOOSE_AFTER:
                                choose(i, h + 1)
                            if h == 0 and g == TAKE_AFTER:
                                dve.wait_ge(y_out, i * 16 + 16)
                                nc.vector.tensor_copy(x1[:], next_x[:]).then_inc(handed, 1)
                            if h == NEXT_UNIT and g == RESIDUAL_AFTER:
                                residual(i + 1, gate1[:])
                            if h == NEXT_UNIT and g == MODULATE_AFTER:
                                modulate(i + 1, gain[:], shift[:])
                    dve.wait_ge(summed, i * U_T + (U_T + RING))
                    dve.wait_ge(gate2_in, i * 16 + 16)
                    nc.vector.tensor_tensor(acc[:], acc[:], gate2[:], ALU.mult)
                    dve.drain()
                    nc.vector.tensor_tensor(x1[:], x1[:], acc[:], ALU.add).then_inc(acc_read, 1)
                    dve.drain()
                    nc.vector.tensor_tensor_reduce(out=h2[:], in0=x1[:], in1=x1[:], scale=1.0, scalar=0.0,
                                                   op0=ALU.mult, op1=ALU.add, accum_out=st[:, 0:1])
                    dve.drain()
                    nc.vector.tensor_scalar(st[:, 1:2], st[:, 0:1], 1.0 / D, EPS, ALU.mult, ALU.add)\
                        .then_inc(p_meansq, 1)
                    dve.wait_ge(p_rooted, i + 1)
                    nc.vector.reciprocal(st[:, 3:4], st[:, 2:3])
                    dve.drain()
                    nc.vector.scalar_tensor_tensor(out=x1[:], in0=x1[:], scalar=st[:, 3:4], in1=gfin[:],
                                                   op0=ALU.mult, op1=ALU.mult).then_inc(y_ready, 1)


def build(nc, t):
    with ExitStack() as ctx:
        def sb(name, shape):
            return ctx.enter_context(nc.sbuf_tensor(name, shape, F32))

        ident = sb("ident", [P, P])
        t["junk"], t["tock"], t["carry"] = sb("junk", [P, 8]), sb("tock", [P, 2]), sb("carry", [P, 3])
        t["ident"] = ident
        started = ctx.enter_context(nc.semaphore("started"))
        with ExitStack() as inner:
            def msb(name, shape):
                return inner.enter_context(nc.sbuf_tensor(name, shape, F32))

            hT = msb("hT", [P, KC, TOK])
            modulation_stage(nc, ctx, t, ident, hT, started)
            neg_u, decay = msb("neg_u", [HEADS, 2, TOK]), msb("decay", [HEADS, 2, TOK])
            cols, masks = msb("cols", [P, 2, 2, NT, HEADS]), msb("masks", [P, 2, P])
            gates_stage(nc, ctx, t, ident, hT, neg_u, decay, cols, masks)
            mixer_stage(nc, ctx, t, ident, hT, neg_u, decay, cols, masks, started)
        peer_stage(nc, ctx, t, ident, started)


def layouts(i):
    import numpy as np
    a = {k: np.asarray(v) for k, v in i.items()}
    w_in = a["w_in"][0]

    def spread(g):
        wide = np.zeros(g.shape[:-1] + (32,), g.dtype)
        wide[..., :HEADS] = g
        return wide.reshape(g.shape[:-2] + (P,))

    out = {
        "x": np.concatenate([a["x_prompt"].reshape(1, P, D), a["x_sample"].reshape(NT - 1, P, D)]),
        "cond": np.stack([a["c_ctx"], a["c"][0]]).reshape(2, KC, P).transpose(2, 1, 0),
        "w_ada": a["w_ada"][0].reshape(KC, P, 12, 512).transpose(2, 1, 0, 3),
        "b_ada": a["b_ada"][0],
        "g_norm1": a["g_norm1"][0], "g_norm2": a["g_norm2"][0], "g_final": a["g_final"],
        "w_in": w_in[:, :3584].reshape(KC, P, KINDS, HEADS, P)[:, :, [1, 2, 0, 3, 4, 5, 6]].transpose(3, 2, 1, 0, 4),
        "w_gate": spread(w_in[:, 3584:].reshape(KC, P, 4, HEADS)).transpose(1, 0, 2),
        "b_gate": spread(np.stack([a["b_igate"][0], a["b_fgate"][0]]).reshape(4, HEADS))[:, None],
        "m0": a["state_m"][0, 0].T,
        "state": np.concatenate([a["state_C"][0, 0], a["state_n"][0, 0][..., None]], axis=-1),
        "conv": np.concatenate([a["conv_w"][0], a["conv_b"]]).reshape(4, 4, P).transpose(2, 1, 0),
        "g_mlstm": a["g_mlstm"][0].T,
        "w_out": a["w_out"][0].reshape(KC, P, D).transpose(1, 0, 2),
        "wq": a["peer_wq"][0].reshape(KC, P, PH * 2 * P).transpose(1, 0, 2),
        "keys": np.stack([a["peer_k1"][0], a["peer_k2"][0]]).transpose(2, 0, 1),
        "uv": np.concatenate([a["peer_u"][0], a["peer_v"][0]], axis=-1),
    }
    return {k: np.ascontiguousarray(v) for k, v in out.items()}


OUTS = {"y": (NT, P, D), "new_C": (2, HEADS, DH, DH), "new_n": (2, HEADS, DH, 1), "new_m": (HEADS, 2)}
SCRATCH = {"mod": (2, 6 * D), "cat": (NT, P, 2 * HEADS, P)}


def kernel(**inputs):
    import concourse.bacc as bacc
    from concourse.bass_utils import run_bass_kernel_spmd as run

    nc = bacc.Bacc("TRN2", target_bir_lowering=False, num_devices=1)
    arrays = layouts(inputs)
    t = {k: nc.dram_tensor(f"in_{k}", a.shape, F32, kind="ExternalInput").ap() for k, a in arrays.items()}
    t.update({k: nc.dram_tensor(f"out_{k}", s, F32, kind="ExternalOutput").ap() for k, s in OUTS.items()})
    t.update({k: nc.dram_tensor(f"scratch_{k}", s, F32).ap() for k, s in SCRATCH.items()})
    build(nc, t)
    r = run(nc, [{f"in_{k}": a for k, a in arrays.items()}], core_ids=[0]).results[0]
    y = r["out_y"]
    return (y[0].reshape(1, P, D), y[1:].reshape(1, (NT - 1) * P, D),
            r["out_new_C"].reshape(1, 1, 2, HEADS, DH, DH), r["out_new_n"].reshape(1, 1, 2, HEADS, DH),
            r["out_new_m"].T.reshape(1, 1, 2, HEADS))
```

```python
from contextlib import ExitStack

import concourse.bass as bass
from concourse import mybir

ALU = mybir.AluOpType
ACT = mybir.ActivationFunctionType
F32 = mybir.dt.float32
U32 = mybir.dt.uint32
X = mybir.AxisListType.X

P = 128
D = 1024
KC = D // P
NT = 9
TOK = NT * P
BANK = 512
HEADS = 4
DH = 128
GRID = 64
PH = 8
TOPK = 16
KEYS = 128
EPS = 1e-6
LOW = -1.0e30
DROPPED = -3.0e38
KINDS = 7
CG, XG, BG, Q, K, V, OG = range(KINDS)
SPANS = [(0, 512), (512, 1024), (1024, TOK)]


def carry_wait(nc, t, engine):
    spot = t["carry"]
    if engine == "act":
        nc.scalar.copy(spot[:, 0:1], t["ident"][:, 0:1])
    elif engine == "pool":
        return nc.gpsimd.tensor_tensor(spot[:, 1:2], t["ident"][:, 0:1], t["ident"][:, 0:1], ALU.add)
    else:
        nc.vector.memset(spot[:, 2:3], 0.0)


def modulation_stage(nc, ctx, t, ident, hT, started):
    PIECES, SLOTS = 12, 4
    FIRST = 2 * D // BANK
    HS = 2
    with ExitStack() as own:
        def sb(name, shape):
            return own.enter_context(nc.sbuf_tensor(name, shape, F32))

        def sem(name):
            return ctx.enter_context(nc.semaphore(name))

        wada = sb("wada", [P, SLOTS, KC, BANK])
        cond, silu = sb("cond", [P, KC, 2]), sb("silu", [P, KC, 2])
        mod = sb("mod", [2, 6 * D])
        xt, ht = sb("xt", [P, SLOTS, D]), sb("ht", [P, HS, D])
        st = sb("st", [P, SLOTS, 4])
        gain, shift, g1 = sb("gain", [P, 2, D]), sb("shift", [P, 2, D]), sb("g1", [P, D])
        pick = sb("pick", [2, 2, P])
        ps_mod = [own.enter_context(nc.psum_tensor(f"ps_mod{j}", [P, BANK], F32)) for j in range(SLOTS)]
        ps = [own.enter_context(nc.psum_tensor(f"psn{j}", [P, 2 * BANK], F32)) for j in range(HS)]
        cond_in, bias_in, g1_in, spread = sem("cond_in"), sem("bias_in"), sem("g1_in"), sem("spread")
        piece_in = [sem(f"piece_in{j}") for j in range(SLOTS)]
        x_in = [sem(f"x_in{j}") for j in range(SLOTS)]
        piece_used, biased, silu_done = sem("piece_used"), sem("biased"), sem("silu_done")
        gain_read, shift_read, mod_out = sem("gain_read"), sem("shift_read"), sem("mod_out")
        meansq, rooted, normed = sem("meansq"), sem("rooted"), sem("normed")
        turned, evicted = sem("turned"), sem("evicted")

        with nc.Block() as block:
            @block.sync
            def _(sp):
                sp.dma_start(cond[:], t["cond"]).then_inc(cond_in, 16)
                sp.dma_start(mod[:], t["b_ada"].partition_broadcast(2)).then_inc(bias_in, 16)
                for j in range(FIRST):
                    sp.dma_start(wada[:, j], t["w_ada"][j]).then_inc(piece_in[j], 16)
                    if j == 1:
                        sp.dma_start(g1[:], t["g_norm1"].partition_broadcast(P)).then_inc(g1_in, 16)

                def load_x(i, j):
                    sp.wait_ge(normed, i * SLOTS + (j + 1))
                    sp.dma_start(xt[:, j], t["x"][i * SLOTS + j]).then_inc(x_in[j], 16)

                with sp.Fori(0, PIECES // SLOTS - 1) as i:
                    for j in range(SLOTS):
                        sp.wait_ge(piece_used, i * SLOTS + (j + 1))
                        sp.dma_start(wada[:, j], t["w_ada"][i * SLOTS + (j + FIRST)]).then_inc(piece_in[j], 16)
                        load_x(i, j)
                load_x(2, 0)
                sp.wait_ge(biased, PIECES)
                sp.dma_start(t["mod"], mod[:]).then_inc(mod_out, 16)
                sp.wait_ge(mod_out, 16)

            @block.gpsimd
            def _(pool):
                nc.gpsimd.memset(t["junk"][:, 0:1], 0.0).then_inc(normed, SLOTS)
                nc.gpsimd.memset(t["junk"][:, 1:2], 0.0).then_inc(turned, HS)
                nc.gpsimd.memset(t["junk"][:, 2:3], 0.0).then_inc(evicted, HS)
                nc.gpsimd.memset(ident[:], 1.0)
                nc.gpsimd.memset(pick[:], 1.0)
                pool.drain()
                nc.gpsimd.affine_select(out=pick[:], in_=pick[:], compare_op=ALU.is_equal, fill=0.0,
                                        base=0, pattern=[[-1, 2], [0, P]], channel_multiplier=1)
                pool.drain()
                nc.gpsimd.affine_select(out=ident[:], in_=ident[:], compare_op=ALU.is_equal, fill=0.0,
                                        base=0, pattern=[[-1, P]], channel_multiplier=1).then_inc(started, 1)

            @block.scalar
            def _(act):
                act.wait_ge(cond_in, 16)
                nc.scalar.activation(silu[:], cond[:], ACT.Silu).then_inc(silu_done, 1)
                for c in range(2):
                    act.wait_ge(spread, 2 * c + 2)
                    nc.scalar.copy(shift[:, c], ps[1][:]).then_inc(shift_read, 1)
                act.wait_ge(started, 1)

                def root_and_evict(i, j):
                    tile = i * SLOTS + j
                    act.wait_ge(meansq, tile + 1)
                    nc.scalar.activation(st[:, j, 2:3], st[:, j, 1:2], ACT.Sqrt).then_inc(rooted, 1)
                    act.drain()
                    act.wait_ge(turned, tile + (1 + HS))
                    carry_wait(nc, t, "act")
                    nc.scalar.copy(hT[:, :, bass.ts(tile, P)],
                                   ps[j % HS][:].rearrange("p (k n) -> p k n", k=KC)).then_inc(evicted, 1)

                with act.Fori(0, NT // SLOTS) as i:
                    for j in range(SLOTS):
                        root_and_evict(i, j)
                root_and_evict(2, 0)

            @block.tensor
            def _(pe):
                def multiply(i, j):
                    pe.wait_ge(piece_in[j], i * 16 + 16)
                    if not isinstance(i, int):
                        pe.wait_ge(biased, (i - 1) * SLOTS + (j + 1))
                    for k in range(KC):
                        last = nc.tensor.matmul(ps_mod[j][0:2, :], silu[:, k, :], wada[:, j, k, :], start=(k == 0),
                                                stop=(k == KC - 1))
                    last.then_inc(piece_used, 1)

                def turn(i, j):
                    pe.wait_ge(normed, i * SLOTS + (j + 1 + SLOTS))
                    pe.wait_ge(evicted, i * SLOTS + (j + 1))
                    for k in range(KC):
                        last = nc.tensor.transpose(ps[j % HS][:, k * P:(k + 1) * P],
                                                   ht[:, j % HS, k * P:(k + 1) * P], ident[:])
                    last.then_inc(turned, 1)

                pe.wait_ge(silu_done, 1)
                for j in range(FIRST):
                    multiply(0, j)
                pe.wait_ge(started, 1)
                pe.wait_ge(biased, FIRST)
                for c in range(2):
                    for slot, v in ((0, 1), (1, 0)):
                        if c:
                            pe.wait_ge((gain_read, shift_read)[slot], 1)
                        for a in range(2):
                            at = v * D + a * BANK
                            last = nc.tensor.matmul(ps[slot][:, a * BANK:(a + 1) * BANK], pick[:, c, :],
                                                    mod[:, at:at + BANK], start=True, stop=True)
                        last.then_inc(spread, 1)
                pe.wait_ge(gain_read, 2)
                pe.wait_ge(shift_read, 2)
                with pe.Fori(0, NT // SLOTS) as i:
                    for step, j in ((multiply, 0), (multiply, 1), (turn, 0), (multiply, 2), (turn, 1), (turn, 2),
                                    (multiply, 3), (turn, 3)):
                        step(i + 1 if step is multiply else i, j)
                turn(2, 0)

            @block.vector
            def _(dve):
                def bias(i, j):
                    dve.wait_ge(piece_used, i * SLOTS + (j + 1))
                    at = mod[:, j * BANK:(j + 1) * BANK] if isinstance(i, int) else \
                        mod[:, bass.ts(i * SLOTS + j, BANK)]
                    nc.vector.tensor_tensor(at, ps_mod[j][0:2, :], at, ALU.add).then_inc(biased, 1)

                def norm(i, j):
                    tile = i * SLOTS + j
                    s = j % HS
                    c = (tile + 7) // 8
                    dve.wait_ge(x_in[j], i * 16 + 16)
                    dve.wait_ge(turned, tile + 1)
                    nc.vector.tensor_tensor_reduce(out=ht[:, s], in0=xt[:, j], in1=xt[:, j], scale=1.0,
                                                   scalar=0.0, op0=ALU.mult, op1=ALU.add,
                                                   accum_out=st[:, j, 0:1])
                    dve.drain()
                    nc.vector.tensor_scalar(st[:, j, 1:2], st[:, j, 0:1], 1.0 / D, EPS, ALU.mult,
                                            ALU.add).then_inc(meansq, 1)
                    dve.wait_ge(rooted, tile + 1)
                    nc.vector.reciprocal(st[:, j, 3:4], st[:, j, 2:3])
                    dve.drain()
                    nc.vector.scalar_tensor_tensor(out=ht[:, s], in0=xt[:, j], scalar=st[:, j, 3:4],
                                                   in1=gain[:, c], op0=ALU.mult, op1=ALU.mult)
                    dve.drain()
                    nc.vector.tensor_tensor(ht[:, s], ht[:, s], shift[:, c], ALU.add).then_inc(normed, 1)

                dve.wait_ge(bias_in, 16)
                for j in range(FIRST):
                    bias(0, j)
                dve.wait_ge(g1_in, 16)
                for c in range(2):
                    dve.wait_ge(spread, 2 * c + 1)
                    nc.vector.scalar_tensor_tensor(out=gain[:, c], in0=ps[0][:], scalar=1.0, in1=g1[:],
                                                   op0=ALU.add, op1=ALU.mult).then_inc(gain_read, 1)
                dve.wait_ge(shift_read, 2)
                dve.drain()
                with dve.Fori(0, NT // SLOTS) as i:
                    for j in range(SLOTS):
                        norm(i, j)
                        bias(i + 1, j)
                norm(2, 0)


def mod_vector(t, cond, v):
    return t["mod"][cond, v * D:(v + 1) * D].partition_broadcast(P)


PROLOGUE = HANDED_ON = ("q", "v", "k")
BODY = ["ktok", "og", "vtok", "s", "u0", "a0", "cg", "kv0", "xg", "num0", "u1", "a1", "k", "kv1", "bg",
        "num1", "q", "v", "hT"]
NJ = len(BODY)
PROJ = {"cg": CG, "xg": XG, "bg": BG, "q": Q, "k": K, "v": V, "og": OG}


def region_of(name):
    return BODY.index(name) % 2


def left_out(h, name, region=None):
    if not isinstance(h, int) or h < HEADS - 1:
        return 0
    return sum(BODY.index(x) < BODY.index(name) and region in (None, region_of(x)) for x in HANDED_ON)


def job_done(h, name):
    return h * NJ + (len(PROLOGUE) + BODY.index(name) + 1 - left_out(h, name))


def region_free(h, name):
    r, j = region_of(name), BODY.index(name)
    before = sum(region_of(x) == r for x in PROLOGUE) + sum(region_of(x) == r for x in BODY[:j])
    return r, h * sum(region_of(x) == r for x in BODY) + (1 + before - left_out(h, name, r))


def region_free_first(name):
    return region_of(name), 1 + sum(region_of(x) == region_of(name) for x in PROLOGUE[:PROLOGUE.index(name)])


def evicted(h, name):
    r, value = region_free(h, name)
    return r, value + 1


def mixer_stage(nc, ctx, t, ident, hT, wo, gfin, wo_in):
    W = DH + 1
    with ExitStack() as own:
        def sb(name, shape):
            return own.enter_context(nc.sbuf_tensor(name, shape, F32))

        def sem(name):
            return ctx.enter_context(nc.semaphore(name))

        w = sb("w", [P, KINDS, KC, P])
        qT, kT, vT, og = (sb(n, [P, TOK]) for n in ("qT", "kT", "vT", "ogT"))
        ktok = sb("ktok", [P, NT, P])
        vtok = sb("vtok", [P, NT, W])
        sT = sb("sT", [P, NT, P])
        seen = sb("seen", [P, NT, P])
        qa = sb("qa", [P, NT, P])
        kw = sb("kw", [P, NT, P])
        states = sb("states", [P, NT, W])
        num = sb("num", [P, NT, W])
        hsum = sb("hsum", [P, NT, P])
        u = sb("u", [P, TOK])
        y = sb("y", [P, TOK])
        dec = sb("dec", [P, NT])
        den = sb("den", [P, 2, NT])
        rows = sb("rows", [HEADS, 2, TOK])
        ones = sb("ones", [HEADS, P])
        new = sb("new", [P, 2, W])
        mixed = sb("mixed_rows", [P, 2, TOK])
        conv = sb("conv", [P, 4, 4])
        gm = sb("gm", [P, HEADS])
        neg_u, decay = sb("neg_u", [HEADS, 2, TOK]), sb("decay", [HEADS, 2, TOK])
        cols, masks = sb("cols", [P, 2, 2, NT, HEADS]), sb("masks", [P, 2, P])
        wg, gb, m0 = sb("wg", [P, KC, P]), sb("gb", [P, 1]), sb("m0", [HEADS, 2])
        keep, low, top = (sb(n, [HEADS, TOK]) for n in ("keep", "low", "top"))
        ends, newm = sb("ends", [HEADS, 3, NT]), sb("newm", [HEADS, 2])

        def lent(tensor):
            return tensor[0:HEADS].rearrange("h c n -> h (c n)")

        gi, gf = [u[0:HEADS, :], y[0:HEADS, :]], [lent(qa), lent(kw)]
        lg, bsum = [lent(hsum), lent(sT)], lent(seen)
        gmb, em = rows, mixed[0:HEADS]
        chunks = lambda a: a.rearrange("h (c n) -> h c n", c=NT)
        ps_cols = own.enter_context(nc.psum_tensor("psgc", [P, BANK], F32))
        region = [own.enter_context(nc.psum_tensor(f"region{r}", [P, 3 * BANK], F32)) for r in range(2)]

        w_in = [sem(f"w_in{k}") for k in range(KINDS)]
        small_in = sem("small_in")
        jobs_done, free = sem("jobs_done"), [sem("region_free0"), sem("region_free1")]
        masked, exped = sem("masked"), sem("exped")
        weighted, ready = sem("k_weighted"), sem("seen_ready")
        h_ready, rooted = sem("h_ready"), sem("h_rooted")
        meansq, state_in = sem("h_meansq"), [sem("state_in0"), sem("state_in1")]
        new_ready, new_out = sem("new_ready"), [sem("new_out0"), sem("new_out1")]
        combined = sem("combined")
        mixed_out = [sem("conv_out"), sem("mlstm_out")]
        g_in, g_proj, g_forget, g_log = sem("g_in"), sem("g_proj"), sem("g_forget"), sem("g_log")
        g_args, g_exp, g_turned, cols_ready = sem("g_args"), sem("g_exp"), sem("g_turned"), sem("cols_ready")
        g_masks, g_out = sem("g_masks"), sem("g_out")

        def wait_evicted(eng, h, name):
            r, value = evicted(h, name)
            eng.wait_ge(free[r], value)

        def reg(name):
            return region[region_of(name)]

        def toks(name):
            return reg(name)[:, 0:TOK]

        def tiles(name):
            return reg(name)[:, 0:TOK].rearrange("p (c n) -> p c n", c=NT)

        def wide(name):
            return reg(name)[:].rearrange("p (b n) -> p b n", b=3)[:, :, 0:3 * W].rearrange(
                "p b (c n) -> p b c n", c=3)

        def wide_at(name, c):
            return reg(name)[:, (c // 3) * BANK + (c % 3) * W:(c // 3) * BANK + (c % 3 + 1) * W]

        with nc.Block() as block:
            @block.sync
            def _(sp):
                for tensor, name in ((wg, "w_gate"), (gb, "b_gate"), (m0, "m0")):
                    sp.dma_start(tensor[:], t[name]).then_inc(g_in, 16)

                def load_w(h, name):
                    sp.dma_start(w[:, PROJ[name]], t["w_in"][h, PROJ[name]]).then_inc(w_in[PROJ[name]], 16)

                def store_new(h, d):
                    sp.wait_ge(new_ready, h * 2 + (d + 1))
                    sp.dma_start(t["new_C"][d, h], new[:, d, 0:DH]).then_inc(new_out[d], 16)
                    sp.dma_start(t["new_n"][d, h], new[:, d, DH:W]).then_inc(new_out[d], 16)

                def store_mixed(h, g, name):
                    wait_evicted(sp, h, name)
                    sp.dma_start(t["cat"][:, :, g * HEADS + h, :].rearrange("n p c -> p n c"),
                                 mixed[:, g].rearrange("p (n c) -> p n c", n=NT)).then_inc(mixed_out[g], 16)

                for name in (*PROLOGUE, "og"):
                    load_w(0, name)
                sp.dma_start(conv[:], t["conv"]).then_inc(small_in, 16)
                sp.dma_start(gm[:], t["g_mlstm"]).then_inc(small_in, 16)
                sp.dma_start(states[:, 1], t["state"][0, 0]).then_inc(state_in[0], 16)
                for name in ("cg", "xg", "bg"):
                    load_w(0, name)
                for j, name in enumerate(PROLOGUE):
                    sp.wait_ge(jobs_done, j + 1)
                    load_w(1, name)
                sp.wait_ge(g_args, 2)
                sp.dma_start(t["new_m"], newm[:]).then_inc(g_out, 16)
                for h in range(HEADS):
                    for name in BODY:
                        to = h + (2 if name in HANDED_ON else 1)
                        if name in PROJ and to < HEADS:
                            sp.wait_ge(jobs_done, job_done(h, name))
                            load_w(to, name)
                        if name in ("bg", "hT"):
                            store_mixed(h, int(name == "hT"), name)
                        if name in ("kv0", "kv1"):
                            store_new(h, int(name[-1]))
                        elif name == "num0":
                            sp.wait_ge(jobs_done, job_done(h, "num0"))
                            sp.dma_start(states[:, NT - 1], t["state"][1, h]).then_inc(state_in[1], 16)
                        elif name == "num1" and h < HEADS - 1:
                            sp.wait_ge(jobs_done, job_done(h, "num1"))
                            sp.dma_start(states[:, 1], t["state"][0, h + 1]).then_inc(state_in[0], 16)
                        elif name == "bg" and h == HEADS - 1:
                            sp.wait_ge(jobs_done, job_done(h, "bg"))
                            for a in range(2):
                                sp.dma_start(wo[:, :, a * BANK:(a + 1) * BANK],
                                             t["w_out"][:, :, a * BANK:(a + 1) * BANK]).then_inc(wo_in[a], 16)
                            sp.dma_start(gfin, t["g_final"].partition_broadcast(P)).then_inc(wo_in[1], 16)
                sp.wait_ge(g_out, 16)
                for d in range(2):
                    sp.wait_ge(new_out[d], 32 + 32 * HEADS)
                    sp.wait_ge(mixed_out[d], 16 + 16 * HEADS)

            @block.gpsimd
            def _(pool):
                nc.gpsimd.memset(ones[:], 1.0)
                nc.gpsimd.memset(vtok[:, :, DH:W], 1.0).then_inc(free[1 - region_of("v")], 1)
                nc.gpsimd.memset(masks[:], 1.0)
                pool.drain()
                nc.gpsimd.affine_select(out=masks[:, 0], in_=masks[:, 0], compare_op=ALU.is_ge, fill=0.0,
                                        base=0, pattern=[[1, P]], channel_multiplier=-1)
                nc.gpsimd.affine_select(out=masks[:, 1], in_=masks[:, 1], compare_op=ALU.is_ge, fill=0.0,
                                        base=0, pattern=[[-1, P]], channel_multiplier=1)
                pool.drain()
                nc.gpsimd.memset(t["junk"][:, 0:1], 1.0).then_inc(g_masks, 1)
                for d in range(2):
                    nc.gpsimd.memset(t["junk"][:, 1 + d:2 + d], 1.0).then_inc(new_out[d], 32)
                    nc.gpsimd.memset(t["junk"][:, 3 + d:4 + d], 1.0).then_inc(mixed_out[d], 16)

            @block.tensor
            def _(pe):
                pe.wait_ge(g_in, 48)
                for a, b in SPANS:
                    for k in range(KC):
                        last = nc.tensor.matmul(region[region_of("v")][:, a:b], wg[:, k, :], hT[:, k, a:b],
                                                start=(k == 0), stop=(k == KC - 1))
                last.then_inc(g_proj, 1)

                def project(name, head, free_at):
                    pe.wait_ge(w_in[PROJ[name]], head * 16 + 16)
                    pe.wait_ge(free[free_at[0]], free_at[1])
                    for k in range(KC):
                        for a, b in SPANS:
                            last = nc.tensor.matmul(reg(name)[:, a:b], w[:, PROJ[name], k, :], hT[:, k, a:b],
                                                    start=(k == 0), stop=(k == KC - 1))
                    last.then_inc(jobs_done, 1)

                for name in PROLOGUE:
                    project(name, 0, region_free_first(name))
                pe.wait_ge(g_exp, 2)
                for d in range(2):
                    for kind, src in enumerate((gmb, em)):
                        for c in range(NT):
                            at = ((d * 2 + kind) * NT + c) * HEADS
                            last = nc.tensor.transpose(ps_cols[:, at:at + HEADS], src[:, d, c * P:(c + 1) * P],
                                                       ident[0:HEADS, 0:HEADS])
                last.then_inc(g_turned, 1)
                for name in PROLOGUE:
                    r, value = region_free_first(name)
                    pe.wait_ge(free[r], value + 1)

                def body(h):
                    def take(name):
                        r, value = region_free(h, name)
                        pe.wait_ge(free[r], value)

                    def project_own(name):
                        project(name, h, region_free(h, name))

                    def project_next(name):
                        if not isinstance(h, int):
                            project(name, h + 1, region_free(h, name))

                    def turn(name, src):
                        for c in range(NT):
                            last = nc.tensor.transpose(tiles(name)[:, c], src[:, c * P:(c + 1) * P], ident[:])
                        last.then_inc(jobs_done, 1)

                    take("ktok")
                    turn("ktok", kT)
                    project_own("og")
                    take("vtok")
                    turn("vtok", vT)
                    take("s")
                    for c in range(NT):
                        last = nc.tensor.matmul(tiles("s")[:, c], kT[:, c * P:(c + 1) * P], qT[:, c * P:(c + 1) * P],
                                                start=True, stop=True)
                    last.then_inc(jobs_done, 1)

                    def spread_rows(d):
                        pe.wait_ge(masked, h * 2 + (d + 1))
                        for kind, name in enumerate((f"u{d}", f"a{d}")):
                            take(name)
                            for a, b in SPANS:
                                last = nc.tensor.matmul(reg(name)[:, a:b], ones[:], rows[:, kind, a:b],
                                                        start=True, stop=True)
                            last.then_inc(jobs_done, 1)

                    def outer(d):
                        pe.wait_ge(weighted, h * 2 + (d + 1))
                        take(f"kv{d}")
                        for c in range(NT):
                            last = nc.tensor.matmul(wide_at(f"kv{d}", c), kw[:, c, :], vtok[:, c, :],
                                                    start=True, stop=True)
                        last.then_inc(jobs_done, 1)

                    def numerators(d):
                        pe.wait_ge(ready, h * 2 + (d + 1))
                        wait_evicted(pe, h, "vtok")
                        wait_evicted(pe, h, f"kv{d}")
                        take(f"num{d}")
                        for c in range(NT):
                            last = nc.tensor.matmul(wide_at(f"num{d}", c), seen[:, c, :], vtok[:, c, :],
                                                    start=True, stop=(c == 0))
                            if c:
                                last = nc.tensor.matmul(wide_at(f"num{d}", c), qa[:, c, :], states[:, c, :],
                                                        start=False, stop=True)
                        last.then_inc(jobs_done, 1)

                    spread_rows(0)
                    project_own("cg")
                    outer(0)
                    project_own("xg")
                    numerators(0)
                    spread_rows(1)
                    project_next("k")
                    outer(1)
                    project_own("bg")
                    numerators(1)
                    project_next("q")
                    project_next("v")
                    pe.wait_ge(h_ready, h + 1)
                    take("hT")
                    for c in range(NT):
                        last = nc.tensor.transpose(tiles("hT")[:, c], hsum[:, c, :], ident[:])
                    last.then_inc(jobs_done, 1)
                    if not isinstance(h, int):
                        for name in HANDED_ON:
                            wait_evicted(pe, h, name)

                with pe.Fori(0, HEADS - 1) as h:
                    body(h)
                body(HEADS - 1)

            @block.scalar
            def _(act):
                EVICT = {"q": (qT, float(DH) ** -0.5), "k": (kT, 1.0), "v": (vT, 1.0)}

                def evict_first(name):
                    out, scale = EVICT[name]
                    act.wait_ge(jobs_done, PROLOGUE.index(name) + 1)
                    nc.scalar.activation(out[:], toks(name), ACT.Copy, scale=scale).then_inc(free[region_of(name)], 1)

                def gate_exps(d):
                    act.wait_ge(g_args, d + 1)
                    nc.scalar.activation(decay[:, d], decay[:, d], ACT.Exp)
                    nc.scalar.activation(em[:, d], em[:, d], ACT.Exp).then_inc(g_exp, 1)

                act.wait_ge(g_forget, 1)
                for step in ((ACT.Abs, 1.0, 0.0), (ACT.Exp, -1.0, 0.0), (ACT.Ln, 1.0, 1.0)):
                    func, scale, bias = step
                    for d in range(2):
                        nc.scalar.activation(lg[d], gf[d] if func == ACT.Abs else lg[d], func, scale=scale, bias=bias)
                    act.drain()
                nc.scalar.copy(t["carry"][:, 0:1], ident[:, 0:1]).then_inc(g_log, 1)
                evict_first("q")
                gate_exps(0)
                evict_first("v")
                gate_exps(1)
                evict_first("k")
                act.wait_ge(g_turned, 1)
                nc.scalar.copy(cols[:].rearrange("p a b c h -> p (a b c h)"), ps_cols[:, 0:16 * NT])\
                    .then_inc(cols_ready, 1)

                def body(h):
                    def evict(name, out, src, func=ACT.Copy, scale=1.0):
                        act.wait_ge(jobs_done, job_done(h, name))
                        nc.scalar.activation(out, src, func, scale=scale).then_inc(free[region_of(name)], 1)

                    def evict_next(name):
                        if not isinstance(h, int):
                            out, scale = EVICT[name]
                            evict(name, out[:], toks(name), scale=scale)

                    evict("ktok", ktok[:], tiles("ktok"))
                    evict("og", og[:], toks("og"), func=ACT.Sigmoid)
                    evict("vtok", vtok[:, :, 0:DH], tiles("vtok"))
                    evict("s", sT[:], tiles("s"))

                    def exps(d):
                        wait_evicted(act, h, f"u{d}")
                        nc.scalar.activation(seen[:], seen[:], ACT.Exp).then_inc(exped, 1)
                        evict(f"a{d}", qa[:], tiles(f"a{d}"))

                    def copy_num(d):
                        if d:
                            act.wait_ge(combined, h * 2 + 2 + 1)
                        act.wait_ge(jobs_done, job_done(h, f"num{d}"))
                        for b in range(3):
                            last = nc.scalar.copy(num[:, 3 * b:3 * b + 3, :], wide(f"num{d}")[:, b])
                        last.then_inc(free[region_of(f"num{d}")], 1)

                    exps(0)
                    evict("cg", u[:], toks("cg"))
                    copy_num(0)
                    exps(1)
                    evict_next("k")
                    copy_num(1)
                    act.wait_ge(ready, h * 2 + 2)
                    evict_next("q")
                    act.wait_ge(meansq, h + 1)
                    nc.scalar.activation(den[:, 1, :], den[:, 0, :], ACT.Sqrt).then_inc(rooted, 1)
                    evict_next("v")

                with act.Fori(0, HEADS - 1) as h:
                    body(h)
                body(HEADS - 1)

            @block.vector
            def _(dve):
                nc.vector.memset(t["tock"][:, 0:2], 0.0).then_inc(combined, 2)
                nc.vector.memset(keep[:], 1.0)
                nc.vector.memset(low[:], 0.0)
                nc.vector.memset(ends[:], 0.0)
                dve.drain()
                nc.vector.memset(chunks(keep[:])[:, :, 0:1], 0.0)
                nc.vector.memset(chunks(low[:])[:, :, 0:1], LOW)
                dve.wait_ge(g_in, 48)
                dve.wait_ge(g_proj, 1)
                for n, out in ((2, gf[0]), (3, gf[1]), (0, gi[0]), (1, gi[1])):
                    at = 32 * n
                    last = nc.vector.tensor_scalar(out, region[region_of("v")][at:at + HEADS, 0:TOK],
                                                   gb[at:at + HEADS, :], None, ALU.add)
                    if n == 3:
                        dve.drain()
                        nc.vector.memset(t["carry"][:, 2:3], 0.0).then_inc(g_forget, 1)
                last.then_inc(free[region_of("v")], 1)
                dve.wait_ge(g_log, 1)
                for d in range(2):
                    nc.vector.scalar_tensor_tensor(out=gf[d], in0=gf[d], scalar=0.0, in1=lg[d], op0=ALU.min,
                                                   op1=ALU.subtract)
                dve.drain()
                for d in range(2):
                    run = (lambda a: a) if d == 0 else (lambda a: a[:, ::-1])
                    end = P - 1 if d == 0 else 0
                    nc.vector.tensor_tensor_scan(out=run(bsum), data0=keep[:], data1=run(gf[d]), initial=0.0,
                                                 op0=ALU.mult, op1=ALU.add)
                    dve.drain()
                    nc.vector.tensor_tensor(gmb[:, d], gi[d], bsum, ALU.subtract)
                    dve.drain()
                    nc.vector.tensor_tensor_scan(out=run(top[:]), data0=low[:], data1=run(gmb[:, d]), initial=0.0,
                                                 op0=ALU.add, op1=ALU.max)
                    dve.drain()
                    nc.vector.memset(ends[:, 2, 0:1], 0.0)
                    nc.vector.tensor_copy(ends[:, 0], chunks(top[:])[:, :, end])
                    nc.vector.tensor_copy(ends[:, 1], chunks(bsum)[:, :, end])
                    first = 1 if d == 0 else NT - 1
                    nc.vector.tensor_copy(ends[:, 2, first:first + 1], m0[:, d:d + 1])
                    dve.drain()
                    nc.vector.scalar_tensor_tensor(out=newm[:, d:d + 1], in0=ends[:, 0, 0:1], scalar=0.0,
                                                   in1=ends[:, 1, 0:1], op0=ALU.max, op1=ALU.add)
                    src = slice(1, NT - 1) if d == 0 else slice(NT - 1, 1, -1)
                    dst = slice(2, NT) if d == 0 else slice(NT - 2, 0, -1)
                    nc.vector.tensor_tensor_scan(out=ends[:, 2, dst], data0=ends[:, 0, src], data1=ends[:, 1, src],
                                                 initial=m0[:, d:d + 1], op0=ALU.max, op1=ALU.add)
                    dve.drain()
                    before = ends[:, 2, :].unsqueeze(2).to_broadcast([HEADS, NT, P])
                    nc.vector.tensor_tensor(chunks(top[:]), chunks(top[:]), before, ALU.max)
                    dve.drain()
                    nc.vector.tensor_scalar(neg_u[:, d], top[:], -1.0, None, ALU.mult)
                    nc.vector.tensor_tensor(chunks(decay[:, d]), before, chunks(top[:]), ALU.subtract)
                    dve.drain()
                    nc.vector.tensor_tensor(em[:, d], neg_u[:, d], bsum, ALU.subtract).then_inc(g_args, 1)
                    dve.drain()
                dve.wait_ge(g_exp, 2)
                dve.wait_ge(g_turned, 1)
                dve.wait_ge(cols_ready, 1)
                dve.wait_ge(g_masks, 1)
                dve.wait_ge(small_in, 32)

                def body(h):
                    def mask_rows(d):
                        if d:
                            dve.wait_ge(jobs_done, job_done(h, "a0"))
                        for kind, src in enumerate((neg_u, decay)):
                            last = nc.vector.tensor_scalar(rows[:, kind], src[:, d], ident[0:HEADS, bass.ds(h, 1)],
                                                           None, ALU.mult)
                        last.then_inc(masked, 1)

                    def arguments(d):
                        dve.wait_ge(jobs_done, job_done(h, f"u{d}"))
                        for c in range(NT):
                            last = nc.vector.tensor_scalar(seen[:, c, :], tiles(f"u{d}")[:, c],
                                                           cols[:, d, 0, c, bass.ds(h, 1)], 0.0, ALU.add, ALU.min)
                        last.then_inc(free[region_of(f"u{d}")], 1)

                    def weights(d):
                        end = P - 1 if d == 0 else 0
                        dve.wait_ge(exped, h * 2 + (d + 1))
                        wait_evicted(dve, h, "ktok")
                        wait_evicted(dve, h, f"a{d}")
                        nc.vector.tensor_copy(dec[:], qa[:, :, end])
                        nc.vector.tensor_tensor(kw[:], ktok[:], seen[:, :, end:end + 1].to_broadcast([P, NT, P]),
                                                ALU.mult).then_inc(weighted, 1)
                        dve.drain()
                        nc.vector.tensor_tensor(qa[:], qa[:], qT[:].rearrange("p (c n) -> p c n", c=NT), ALU.mult)
                        nc.vector.tensor_tensor(seen[:], seen[:],
                                                masks[:, d, :].unsqueeze(1).to_broadcast([P, NT, P]), ALU.mult)
                        dve.drain()
                        nc.vector.tensor_tensor(seen[:], seen[:], sT[:], ALU.mult).then_inc(ready, 1)

                    def chain(d):
                        dve.wait_ge(state_in[d], h * 16 + 16)
                        dve.wait_ge(jobs_done, job_done(h, f"kv{d}"))
                        dve.wait_ge(new_out[d], h * 32 + 32)
                        nc.vector.tensor_copy(new[:, d], wide_at(f"kv{d}", 0)).then_inc(new_ready, 1)
                        order = list(range(1, NT - 1)) if d == 0 else list(range(NT - 1, 1, -1))
                        for c in order:
                            last = nc.vector.scalar_tensor_tensor(out=states[:, c + 1 if d == 0 else c - 1],
                                                           in0=states[:, c], scalar=dec[:, c:c + 1],
                                                           in1=wide_at(f"kv{d}", c), op0=ALU.mult, op1=ALU.add)
                            if c == order[-1]:
                                last.then_inc(free[region_of(f"kv{d}")], 1)
                            dve.drain()

                    def combine(d):
                        wait_evicted(dve, h, f"num{d}")
                        nc.vector.scalar_tensor_tensor(out=den[:, 0, :], in0=num[:, :, DH], scalar=-1.0,
                                                       in1=num[:, :, DH], op0=ALU.mult, op1=ALU.max)
                        dve.drain()
                        nc.vector.tensor_tensor(den[:, 0, :], den[:, 0, :], cols[:, d, 1, :, h], ALU.max)
                        dve.drain()
                        nc.vector.reciprocal(den[:, 1, :], den[:, 0, :])
                        dve.drain()
                        r = den[:, 1, :].unsqueeze(2).to_broadcast([P, NT, P])
                        if d == 0:
                            nc.vector.tensor_tensor(hsum[:], num[:, :, 0:DH], r, ALU.mult).then_inc(combined, 1)
                        else:
                            nc.vector.tensor_tensor(num[:, :, 0:DH], num[:, :, 0:DH], r, ALU.mult)
                            dve.drain()
                            nc.vector.tensor_tensor(hsum[:], hsum[:], num[:, :, 0:DH], ALU.add)\
                                .then_inc(combined, 1)
                        dve.drain()

                    mask_rows(0)
                    arguments(0)
                    weights(0)
                    mask_rows(1)
                    chain(0)
                    dve.wait_ge(jobs_done, job_done(h, "xg"))
                    nc.vector.tensor_tensor(u[:], toks("xg"), u[:], ALU.mult)\
                        .then_inc(free[region_of("xg")], 1)
                    combine(0)
                    arguments(1)
                    weights(1)

                    nc.vector.tensor_scalar(y[:], u[:], conv[:, h, 1:2], conv[:, h, 3:4], ALU.mult, ALU.add)
                    dve.drain()
                    for tap, (to, frm) in ((0, (slice(1, None), slice(0, -1))), (2, (slice(0, -1), slice(1, None)))):
                        for a, b, n in ((0, P, P), (P, TOK, GRID)):
                            yr = y[:, a:b].rearrange("p (r n) -> p r n", n=n)
                            ur = u[:, a:b].rearrange("p (r n) -> p r n", n=n)
                            nc.vector.scalar_tensor_tensor(out=yr[:, :, to], in0=ur[:, :, frm],
                                                           scalar=conv[:, h, tap:tap + 1], in1=yr[:, :, to],
                                                           op0=ALU.mult, op1=ALU.add)
                        dve.drain()
                    chain(1)
                    dve.wait_ge(jobs_done, job_done(h, "bg"))
                    dve.wait_ge(mixed_out[0], h * 16 + 16)
                    nc.vector.tensor_tensor(mixed[:, 0], toks("bg"), y[:], ALU.mult)\
                        .then_inc(free[region_of("bg")], 1)

                    combine(1)
                    nc.vector.tensor_tensor(kw[:], hsum[:], hsum[:], ALU.mult)
                    dve.drain()
                    nc.vector.tensor_reduce(den[:, 1, :], kw[:], X, ALU.add)
                    dve.drain()
                    nc.vector.tensor_scalar(den[:, 0, :], den[:, 1, :], 1.0 / DH, EPS, ALU.mult, ALU.add)\
                        .then_inc(meansq, 1)
                    dve.wait_ge(rooted, h + 1)
                    nc.vector.reciprocal(den[:, 0, :], den[:, 1, :])
                    dve.drain()
                    nc.vector.tensor_tensor(hsum[:], hsum[:], den[:, 0, :].unsqueeze(2).to_broadcast([P, NT, P]),
                                            ALU.mult).then_inc(h_ready, 1)
                    dve.wait_ge(jobs_done, job_done(h, "hT"))
                    dve.wait_ge(mixed_out[1], h * 16 + 16)
                    nc.vector.scalar_tensor_tensor(out=mixed[:, 1], in0=toks("hT"), scalar=gm[:, bass.ds(h, 1)],
                                                   in1=og[:], op0=ALU.mult, op1=ALU.mult)\
                        .then_inc(free[region_of("hT")], 1)

                with dve.Fori(0, HEADS - 1) as h:
                    body(h)
                body(HEADS - 1)


def peer_stage(nc, ctx, t, ident, wo, gfin, wo_in):
    RING = 8
    DIAG = 2
    UNIT = TOPK
    GROUP = 2
    GROUPS = UNIT // GROUP
    CHOOSE_AFTER, SOFTEN_AFTER = (2, 3, 4), 5
    TAKE_AFTER = 3
    MIX_UNITS, MIX_AFTER = (1, 2, 3, 4), 5
    NEXT_UNIT, RESIDUAL_AFTER, MODULATE_AFTER = 5, 5, 7
    TURN_UNIT, TURN_AFTER = 6, 3
    with ExitStack() as own:
        def sb(name, shape, dt=F32):
            return own.enter_context(nc.sbuf_tensor(name, shape, dt))

        def psum(name, shape):
            return own.enter_context(nc.psum_tensor(name, shape, F32))

        def sem(name):
            return ctx.enter_context(nc.semaphore(name))

        wq = sb("wq", [P, KC, PH * 2 * P])
        keys = sb("keys", [P, 2, KEYS])
        uv = sb("uv", [P, RING, 2 * D])
        h2, h2T, x1 = sb("h2", [P, D]), sb("h2T", [P, KC, P]), sb("x1", [P, D])
        next_x, next_h = sb("next_x", [P, D]), sb("next_h", [P, D])
        cat = next_h[:].rearrange("p (k n) -> p k n", k=KC)
        gate1, gain, shift = sb("gate1", [P, D]), sb("gain2", [P, D]), sb("shift2", [P, D])
        gate2 = sb("gate2", [P, D])
        g2, gate1_c, gain_c, shift_c = uv[:, 0, 0:D], uv[:, 0, D:], uv[:, 1, 0:D], uv[:, 1, D:]
        qs = sb("qs", [P, 2, P])
        sc = qs
        val, ind = sb("val", [P, 2, TOPK]), sb("ind", [P, 2, TOPK], U32)
        work = sb("work", [P, 2 * TOPK * TOPK])
        cand, cand2 = work[:, 0:TOPK * TOPK], work[:, TOPK * TOPK:]
        sc2 = work[:, TOPK * TOPK:].rearrange("p (s k) -> p s k", s=2)
        onehot = work[:].rearrange("p (k j) -> p k j", j=TOPK)
        best, pos = sb("best", [P, TOPK]), sb("pos", [P, TOPK], U32)
        where = sb("where", [P, 2, TOPK], U32)
        picked = sb("picked", [P, 2, TOPK])
        iota = sb("iota", [P, TOPK])
        expert = sb("expert", [P, 2, TOPK], U32)
        low = sb("neg_best", [P, 1])
        ex, z, rz = sb("ex", [P, 2, TOPK]), sb("z", [P, 2]), sb("rz", [P, 2])
        dot, gelu, wt = sb("dot", [P, 2, TOPK]), sb("gelu", [P, 2, TOPK]), sb("wt", [P, 2, TOPK])
        diag = sb("diag", [P, DIAG, P])
        st, next_st = sb("p_st", [P, 4]), sb("next_st", [P, 4])
        acc, ps_q, ps_s = psum("acc", [P, 2 * BANK]), psum("ps_q", [P, 2, P]), psum("ps_s", [P, 2, KEYS])
        mix, ps_t = psum("mix", [P, 2 * BANK]), psum("ps_t", [P, 2 * BANK])

        first_in, fixed_in = sem("first_in"), sem("fixed_in")
        context_in, latent_in = sem("context_in"), sem("latent_in")
        x_in, cat_in, gate2_in = sem("next_x_in"), sem("cat_in"), sem("gate2_in")
        mixed, mix_read, next_meansq, next_rooted = sem("mixed"), sem("mix_read"), sem("n_meansq"), sem("n_rooted")
        normed, turned, h2T_ready, handed = sem("h2_ready"), sem("h2_turned"), sem("h2T_ready"), sem("handed")
        rows_in = [sem(f"rows_in{s}") for s in range(RING)]
        q_done, q_copied, s_done, s_copied = sem("q_done"), sem("q_copied"), sem("s_done"), sem("s_copied")
        chosen, softened = sem("chosen"), sem("softened")
        dotted, gelued, weighed = sem("dotted"), sem("gelued"), sem("weighed")
        diagonal, summed = sem("diagonal"), sem("summed")
        acc_read = sem("acc_read")
        p_meansq, p_rooted, y_ready, y_out = sem("p_meansq"), sem("p_rooted"), sem("y_ready"), sem("y_out")
        carried = sem("p_carried")
        U_T = PH * UNIT
        G_T = PH * GROUPS

        with nc.Block() as block:
            @block.sync
            def _(sp):
                sp.dma_start(cat, t["cat"][0]).then_inc(cat_in, 16)
                sp.dma_start(next_x[:], t["x"][0]).then_inc(x_in, 16)
                sp.dma_start(g2, t["g_norm2"].partition_broadcast(P)).then_inc(context_in, 16)
                for vector, v in ((gate1_c, 2), (gain_c, 4), (shift_c, 3)):
                    sp.dma_start(vector, mod_vector(t, 0, v)).then_inc(context_in, 16)
                sp.dma_start(wq[:, :, 0:2 * P], t["wq"][:, :, 0:2 * P]).then_inc(first_in, 16)
                sp.dma_start(keys[:], t["keys"]).then_inc(first_in, 16)
                for vector, v in ((gate1, 2), (gain, 4), (shift, 3)):
                    sp.dma_start(vector[:], mod_vector(t, 1, v)).then_inc(latent_in, 16)
                sp.dma_start(wq[:, :, 2 * P:], t["wq"][:, :, 2 * P:]).then_inc(fixed_in, 16)
                with sp.Fori(0, NT) as i:
                    sp.wait_ge(acc_read, i + 1)
                    sp.dma_start(gate2[:], t["mod"][(i + 7) // 8, 5 * D:6 * D].partition_broadcast(P))\
                        .then_inc(gate2_in, 16)
                    after = (i + 2) * (NT - 1) // NT
                    sp.wait_ge(handed, i + 1)
                    sp.dma_start(next_x[:], t["x"][after]).then_inc(x_in, 16)
                    sp.wait_ge(turned, i + 1)
                    sp.dma_start(cat, t["cat"][after]).then_inc(cat_in, 16)
                    sp.wait_ge(y_ready, i + 1)
                    sp.dma_start(t["y"][i], x1[:]).then_inc(y_out, 16)
                sp.wait_ge(y_out, 16 + 16 * NT)

            @block.gpsimd
            def _(pool):
                nc.gpsimd.iota(iota[:], pattern=[[1, TOPK]], base=0, channel_multiplier=0,
                               allow_small_or_imprecise_dtypes=True)
                nc.gpsimd.memset(t["junk"][:, 0:1], 0.0).then_inc(carried, 1)
                nc.gpsimd.memset(t["junk"][:, 1:2], 0.0).then_inc(summed, RING)
                pool.drain()
                nc.gpsimd.memset(t["junk"][:, 2:3], 0.0).then_inc(y_out, 16)
                nc.gpsimd.memset(t["junk"][:, 3:4], 0.0).then_inc(acc_read, 1)
                with pool.Fori(0, NT) as i:
                    for h in range(PH):
                        for k in range(UNIT):
                            if k % GROUP == 0:
                                pool.wait_ge(chosen, i * PH + (h + 1))
                                pool.wait_ge(carried, i * G_T + (h * GROUPS + k // GROUP + 1))
                                pool.wait_ge(summed, i * U_T + (h * UNIT + k + GROUP))
                                carry_wait(nc, t, "pool").then_inc(carried, 1)
                            nc.gpsimd.indirect_dma_start(
                                out=uv[:, k % RING, :], out_offset=None, in_=t["uv"],
                                in_offset=bass.IndirectOffsetOnAxis(ap=expert[:, h % 2, k:k + 1], axis=0),
                            ).then_inc(rows_in[k % RING], 16)

            @block.tensor
            def _(pe):
                def query(i, h):
                    if h in (0, PH):
                        pe.wait_ge(h2T_ready, i + (1 if h == 0 else 2))
                    c = h % PH
                    for half in range(2):
                        for k in range(KC):
                            at = (2 * c + half) * P
                            last = nc.tensor.matmul(ps_q[:, half, :], wq[:, k, at:at + P],
                                                    h2T[:, k, :], start=(k == 0), stop=(k == KC - 1))
                    last.then_inc(q_done, 1)

                def score(i, h):
                    pe.wait_ge(q_copied, i * PH + (h + 1))
                    if not isinstance(i, int):
                        pe.wait_ge(s_copied, i * PH + h)
                    for half in range(2):
                        last = nc.tensor.matmul(ps_s[:, half, :], qs[:, half, :], keys[:, half, :], start=True,
                                                stop=True)
                    last.then_inc(s_done, 1)

                def mix_quarter(n, quarter):
                    a, part = divmod(quarter, 2)
                    if quarter == 0:
                        pe.wait_ge(cat_in, n * 16 + 16)
                        if not isinstance(n, int):
                            pe.wait_ge(mix_read, n)
                    for k in range(part * KC // 2, (part + 1) * KC // 2):
                        last = nc.tensor.matmul(mix[:, a * BANK:(a + 1) * BANK], cat[:, k, :],
                                                wo[:, k, a * BANK:(a + 1) * BANK], start=(k == 0),
                                                stop=(k == KC - 1))
                    if part:
                        last.then_inc(mixed, 1)

                def turn(n):
                    pe.wait_ge(normed, n + 1)
                    if not isinstance(n, int):
                        pe.wait_ge(h2T_ready, n)
                    for k in range(KC):
                        last = nc.tensor.transpose(ps_t[:, k * P:(k + 1) * P], next_h[:, k * P:(k + 1) * P], ident[:])
                    last.then_inc(turned, 1)

                for quarter in range(4):
                    pe.wait_ge(wo_in[quarter // 2], 16 + 16 * (quarter // 2))
                    mix_quarter(0, quarter)
                turn(0)
                pe.wait_ge(first_in, 2 * 16)
                query(0, 0)
                score(0, 0)
                pe.wait_ge(fixed_in, 16)
                with pe.Fori(0, NT) as i:
                    for h in range(PH):
                        query(i, h + 1)
                        if h == 0:
                            pe.wait_ge(acc_read, i + 1)
                        for k in range(UNIT):
                            pe.wait_ge(rows_in[k % RING], i * (16 * PH * UNIT // RING)
                                       + 16 * (h * (UNIT // RING) + k // RING + 1))
                            pe.wait_ge(diagonal, i * U_T + (h * UNIT + k + 1))
                            for a in range(2):
                                last = nc.tensor.matmul(acc[:, a * BANK:(a + 1) * BANK], diag[:, k % DIAG, :],
                                                        uv[:, k % RING, D + a * BANK:D + (a + 1) * BANK],
                                                        start=(h == 0 and k == 0),
                                                        stop=(h == PH - 1 and k == UNIT - 1))
                            last.then_inc(summed, 1)
                            if k == GROUP - 1:
                                score(i, h + 1)
                            if h in MIX_UNITS and k == (MIX_AFTER + 1) * GROUP - 1:
                                mix_quarter(i + 1, MIX_UNITS.index(h))
                            if h == TURN_UNIT and k == (TURN_AFTER + 1) * GROUP - 1:
                                turn(i + 1)

            @block.scalar
            def _(act):
                def query(i, h):
                    act.wait_ge(q_done, i * PH + (h + 1))
                    if h or not isinstance(i, int):
                        act.wait_ge(chosen, i * PH + h)
                    nc.scalar.copy(qs[:], ps_q[:]).then_inc(q_copied, 1)

                def scores(i, h):
                    act.wait_ge(s_done, i * PH + (h + 1))
                    nc.scalar.copy(sc[:], ps_s[:]).then_inc(s_copied, 1)

                def soften(i, h):
                    act.wait_ge(chosen, i * PH + (h + 1))
                    nc.scalar.activation(ex[:, h % 2], best[:], ACT.Exp, bias=low[:],
                                         accum_out=z[:, h % 2:h % 2 + 1]).then_inc(softened, 1)

                def root_next(n):
                    act.wait_ge(next_meansq, n + 1)
                    nc.scalar.activation(next_st[:, 2:3], next_st[:, 1:2], ACT.Sqrt).then_inc(next_rooted, 1)

                def evict_h2T(n):
                    act.wait_ge(turned, n + 1)
                    nc.scalar.copy(h2T[:], ps_t[:].rearrange("p (k n) -> p k n", k=KC)).then_inc(h2T_ready, 1)

                root_next(0)
                evict_h2T(0)
                query(0, 0)
                scores(0, 0)
                soften(0, 0)
                with act.Fori(0, NT) as i:
                    for h in range(PH):
                        for g in range(GROUPS):
                            ks = slice(g * GROUP, (g + 1) * GROUP)
                            act.wait_ge(dotted, i * G_T + (h * GROUPS + g + 1))
                            nc.scalar.activation(gelu[:, h % 2, ks], dot[:, h % 2, ks], ACT.Gelu).then_inc(gelued, 1)
                            act.wait_ge(weighed, i * G_T + (h * GROUPS + g + 1))
                            for k in range(g * GROUP, (g + 1) * GROUP):
                                act.wait_ge(summed, i * U_T + (h * UNIT + k + 1 + RING - DIAG))
                                nc.scalar.activation(diag[:, k % DIAG, :], ident[:], ACT.Copy,
                                                     scale=wt[:, h % 2, k:k + 1]).then_inc(diagonal, 1)
                            if g == 0:
                                query(i, h + 1)
                            if g == 1:
                                scores(i, h + 1)
                            if g == SOFTEN_AFTER:
                                soften(i, h + 1)
                            if h == NEXT_UNIT and g == RESIDUAL_AFTER + 1:
                                root_next(i + 1)
                            if h == TURN_UNIT and g == TURN_AFTER + 1:
                                evict_h2T(i + 1)
                    act.wait_ge(p_meansq, i + 1)
                    nc.scalar.activation(st[:, 2:3], st[:, 1:2], ACT.Sqrt).then_inc(p_rooted, 1)

            @block.vector
            def _(dve):
                def choose_halves(i, h):
                    dve.drain()
                    dve.wait_ge(s_copied, i * PH + (h + 1))
                    carry_wait(nc, t, "dve")
                    nc.vector.max(val[:, 0, 0:8], sc[:, 0])
                    nc.vector.max(val[:, 1, 0:8], sc[:, 1])
                    dve.drain()
                    for s in range(2):
                        nc.vector.max_index(ind[:, s, 0:8], val[:, s, 0:8], sc[:, s])
                        nc.vector.match_replace(sc2[:, s, :], val[:, s, 0:8], sc[:, s], DROPPED)
                    dve.drain()
                    nc.vector.max(val[:, 0, 8:16], sc2[:, 0, :])
                    nc.vector.max(val[:, 1, 8:16], sc2[:, 1, :])
                    dve.drain()
                    for s in range(2):
                        nc.vector.max_index(ind[:, s, 8:16], val[:, s, 8:16], sc2[:, s, :])

                def choose_sums(i, h):
                    dve.drain()
                    nc.vector.tensor_tensor(cand.rearrange("p (a b) -> p a b", a=TOPK),
                                            val[:, 0, :].unsqueeze(2).to_broadcast([P, TOPK, TOPK]),
                                            val[:, 1, :].unsqueeze(1).to_broadcast([P, TOPK, TOPK]), ALU.add)
                    dve.drain()
                    if not (isinstance(i, int) and h == 0):
                        dve.wait_ge(softened, i * PH + h)
                        carry_wait(nc, t, "dve")
                    nc.vector.max(best[:, 0:8], cand)
                    dve.drain()
                    nc.vector.max_index(pos[:, 0:8], best[:, 0:8], cand)
                    nc.vector.match_replace(cand2, best[:, 0:8], cand, DROPPED)
                    dve.drain()
                    nc.vector.max(best[:, 8:16], cand2)
                    dve.drain()
                    nc.vector.max_index(pos[:, 8:16], best[:, 8:16], cand2)
                    nc.vector.tensor_scalar(low[:], best[:, 0:1], -1.0, None, ALU.mult)

                def choose_experts(i, h):
                    dve.drain()
                    nc.vector.tensor_scalar(where[:, 0], pos[:], 4, None, ALU.logical_shift_right)
                    nc.vector.tensor_scalar(where[:, 1], pos[:], TOPK - 1, None, ALU.bitwise_and)
                    dve.drain()
                    flat = where[:].rearrange("p s k -> p (s k)")
                    nc.vector.tensor_tensor(onehot, iota[:].unsqueeze(1).to_broadcast([P, 2 * TOPK, TOPK]),
                                            flat.unsqueeze(2).to_broadcast([P, 2 * TOPK, TOPK]), ALU.is_equal)
                    dve.drain()
                    by_side = onehot.rearrange("p (s k) j -> p s k j", s=2)
                    nc.vector.tensor_tensor(by_side, by_side,
                                            ind[:].unsqueeze(2).to_broadcast([P, 2, TOPK, TOPK]), ALU.mult)
                    dve.drain()
                    nc.vector.tensor_reduce(picked[:].rearrange("p s k -> p (s k)"), onehot, X, ALU.add)
                    dve.drain()
                    nc.vector.scalar_tensor_tensor(out=expert[:, h % 2, :], in0=picked[:, 0], scalar=float(KEYS),
                                                   in1=picked[:, 1], op0=ALU.mult, op1=ALU.add).then_inc(chosen, 1)

                def weigh(i, h, g):
                    ks = slice(g * GROUP, (g + 1) * GROUP)
                    if g == 0:
                        dve.wait_ge(softened, i * PH + (h + 1))
                        nc.vector.reciprocal(rz[:, h % 2:h % 2 + 1], z[:, h % 2:h % 2 + 1])
                        dve.drain()
                    dve.wait_ge(gelued, i * G_T + (h * GROUPS + g + 1))
                    nc.vector.scalar_tensor_tensor(out=wt[:, h % 2, ks], in0=gelu[:, h % 2, ks],
                                                   scalar=rz[:, h % 2:h % 2 + 1], in1=ex[:, h % 2, ks],
                                                   op0=ALU.mult, op1=ALU.mult).then_inc(weighed, 1)

                def residual(n, gate1):
                    dve.wait_ge(mixed, n * 2 + 2)
                    nc.vector.tensor_tensor(next_h[:], mix[:], gate1, ALU.mult).then_inc(mix_read, 1)
                    dve.drain()
                    dve.wait_ge(x_in, n * 16 + 16)
                    nc.vector.tensor_tensor(next_x[:], next_x[:], next_h[:], ALU.add)
                    dve.drain()
                    nc.vector.tensor_tensor_reduce(out=next_h[:], in0=next_x[:], in1=next_x[:], scale=1.0, scalar=0.0,
                                                   op0=ALU.mult, op1=ALU.add, accum_out=next_st[:, 0:1])
                    dve.drain()
                    nc.vector.tensor_scalar(next_st[:, 1:2], next_st[:, 0:1], 1.0 / D, EPS, ALU.mult, ALU.add)\
                        .then_inc(next_meansq, 1)

                def modulate(n, gain, shift):
                    dve.wait_ge(next_rooted, n + 1)
                    nc.vector.reciprocal(next_st[:, 3:4], next_st[:, 2:3])
                    dve.drain()
                    nc.vector.scalar_tensor_tensor(out=next_h[:], in0=next_x[:], scalar=next_st[:, 3:4], in1=gain,
                                                   op0=ALU.mult, op1=ALU.mult)
                    dve.drain()
                    nc.vector.tensor_tensor(next_h[:], next_h[:], shift, ALU.add).then_inc(normed, 1)

                dve.wait_ge(y_out, 16)
                dve.wait_ge(context_in, 4 * 16)
                nc.vector.scalar_tensor_tensor(out=gain_c, in0=gain_c, scalar=1.0, in1=g2, op0=ALU.add, op1=ALU.mult)
                residual(0, gate1_c)
                modulate(0, gain_c, shift_c)
                dve.wait_ge(latent_in, 3 * 16)
                nc.vector.scalar_tensor_tensor(out=gain[:], in0=gain[:], scalar=1.0, in1=g2, op0=ALU.add, op1=ALU.mult)
                CHOICE = (choose_halves, choose_sums, choose_experts)
                for step in CHOICE:
                    step(0, 0)
                with dve.Fori(0, NT) as i:
                    nc.vector.tensor_copy(h2[:], next_h[:])
                    dve.drain()
                    for h in range(PH):
                        for g in range(GROUPS):
                            for k in range(g * GROUP, (g + 1) * GROUP):
                                dve.wait_ge(rows_in[k % RING], i * (16 * PH * UNIT // RING)
                                            + 16 * (h * (UNIT // RING) + k // RING + 1))
                                last = nc.vector.tensor_tensor_reduce(
                                    out=uv[:, k % RING, 0:D], in0=uv[:, k % RING, 0:D], in1=h2[:], scale=1.0,
                                    scalar=0.0, op0=ALU.mult, op1=ALU.add, accum_out=dot[:, h % 2, k:k + 1])
                            last.then_inc(dotted, 1)
                            weigh(i, h, g)
                            if g in CHOOSE_AFTER:
                                CHOICE[CHOOSE_AFTER.index(g)](i, h + 1)
                            if h == 0 and g == TAKE_AFTER:
                                dve.wait_ge(y_out, i * 16 + 16)
                                nc.vector.tensor_copy(x1[:], next_x[:]).then_inc(handed, 1)
                            if h == NEXT_UNIT and g == RESIDUAL_AFTER:
                                residual(i + 1, gate1[:])
                            if h == NEXT_UNIT and g == MODULATE_AFTER:
                                modulate(i + 1, gain[:], shift[:])
                    dve.wait_ge(summed, i * U_T + (U_T + RING))
                    dve.wait_ge(gate2_in, i * 16 + 16)
                    nc.vector.tensor_tensor(acc[:], acc[:], gate2[:], ALU.mult)
                    dve.drain()
                    nc.vector.tensor_tensor(x1[:], x1[:], acc[:], ALU.add).then_inc(acc_read, 1)
                    dve.drain()
                    nc.vector.tensor_tensor_reduce(out=h2[:], in0=x1[:], in1=x1[:], scale=1.0, scalar=0.0,
                                                   op0=ALU.mult, op1=ALU.add, accum_out=st[:, 0:1])
                    dve.drain()
                    nc.vector.tensor_scalar(st[:, 1:2], st[:, 0:1], 1.0 / D, EPS, ALU.mult, ALU.add)\
                        .then_inc(p_meansq, 1)
                    dve.wait_ge(p_rooted, i + 1)
                    nc.vector.reciprocal(st[:, 3:4], st[:, 2:3])
                    dve.drain()
                    nc.vector.scalar_tensor_tensor(out=x1[:], in0=x1[:], scalar=st[:, 3:4], in1=gfin,
                                                   op0=ALU.mult, op1=ALU.mult).then_inc(y_ready, 1)


def build(nc, t):
    with ExitStack() as ctx:
        def sb(name, shape):
            return ctx.enter_context(nc.sbuf_tensor(name, shape, F32))

        ident = sb("ident", [P, P])
        t["junk"], t["tock"], t["carry"] = sb("junk", [P, 8]), sb("tock", [P, 2]), sb("carry", [P, 3])
        t["ident"] = ident
        started = ctx.enter_context(nc.semaphore("started"))
        place = sb("hT_then_w_out", [P, KC * TOK])
        hT = place[:].rearrange("p (k n) -> p k n", k=KC)
        wo = place[:, 0:KC * D].rearrange("p (k n) -> p k n", k=KC)
        gfin = place[:, KC * D:(KC + 1) * D]
        wo_in = [ctx.enter_context(nc.semaphore(f"wo_in{a}")) for a in range(2)]
        modulation_stage(nc, ctx, t, ident, hT, started)
        mixer_stage(nc, ctx, t, ident, hT, wo, gfin, wo_in)
        peer_stage(nc, ctx, t, ident, wo, gfin, wo_in)


def layouts(i):
    import numpy as np
    a = {k: np.asarray(v) for k, v in i.items()}
    w_in = a["w_in"][0]

    def spread(g):
        wide = np.zeros(g.shape[:-1] + (32,), g.dtype)
        wide[..., :HEADS] = g
        return wide.reshape(g.shape[:-2] + (P,))

    out = {
        "x": np.concatenate([a["x_prompt"].reshape(1, P, D), a["x_sample"].reshape(NT - 1, P, D)]),
        "cond": np.stack([a["c_ctx"], a["c"][0]]).reshape(2, KC, P).transpose(2, 1, 0),
        "w_ada": a["w_ada"][0].reshape(KC, P, 12, 512).transpose(2, 1, 0, 3),
        "b_ada": a["b_ada"][0],
        "g_norm1": a["g_norm1"][0], "g_norm2": a["g_norm2"][0], "g_final": a["g_final"],
        "w_in": w_in[:, :3584].reshape(KC, P, KINDS, HEADS, P)[:, :, [1, 2, 0, 3, 4, 5, 6]].transpose(3, 2, 1, 0, 4),
        "w_gate": spread(w_in[:, 3584:].reshape(KC, P, 4, HEADS)).transpose(1, 0, 2),
        "b_gate": spread(np.stack([a["b_igate"][0], a["b_fgate"][0]]).reshape(4, HEADS))[:, None],
        "m0": a["state_m"][0, 0].T,
        "state": np.concatenate([a["state_C"][0, 0], a["state_n"][0, 0][..., None]], axis=-1),
        "conv": np.concatenate([a["conv_w"][0], a["conv_b"]]).reshape(4, 4, P).transpose(2, 1, 0),
        "g_mlstm": a["g_mlstm"][0].T,
        "w_out": a["w_out"][0].reshape(KC, P, D).transpose(1, 0, 2),
        "wq": a["peer_wq"][0].reshape(KC, P, PH * 2 * P).transpose(1, 0, 2),
        "keys": np.stack([a["peer_k1"][0], a["peer_k2"][0]]).transpose(2, 0, 1),
        "uv": np.concatenate([a["peer_u"][0], a["peer_v"][0]], axis=-1),
    }
    return {k: np.ascontiguousarray(v) for k, v in out.items()}


OUTS = {"y": (NT, P, D), "new_C": (2, HEADS, DH, DH), "new_n": (2, HEADS, DH, 1), "new_m": (HEADS, 2)}
SCRATCH = {"mod": (2, 6 * D), "cat": (NT, P, 2 * HEADS, P)}


def kernel(**inputs):
    import concourse.bacc as bacc
    from concourse.bass_utils import run_bass_kernel_spmd as run

    nc = bacc.Bacc("TRN2", target_bir_lowering=False, num_devices=1)
    arrays = layouts(inputs)
    t = {k: nc.dram_tensor(f"in_{k}", a.shape, F32, kind="ExternalInput").ap() for k, a in arrays.items()}
    t.update({k: nc.dram_tensor(f"out_{k}", s, F32, kind="ExternalOutput").ap() for k, s in OUTS.items()})
    t.update({k: nc.dram_tensor(f"scratch_{k}", s, F32).ap() for k, s in SCRATCH.items()})
    build(nc, t)
    r = run(nc, [{f"in_{k}": a for k, a in arrays.items()}], core_ids=[0]).results[0]
    y = r["out_y"]
    return (y[0].reshape(1, P, D), y[1:].reshape(1, (NT - 1) * P, D),
            r["out_new_C"].reshape(1, 1, 2, HEADS, DH, DH), r["out_new_n"].reshape(1, 1, 2, HEADS, DH),
            r["out_new_m"].T.reshape(1, 1, 2, HEADS))
```
